# Optimizing a Trainium2 kernel written in Bass

```python
import math
import jax
import jax.numpy as jnp
from jax import lax
import numpy as np

D_MODEL = 1024
BATCH = 1
SEQ = 2048
DEPTH = 2

N_MIXERS = 2
RMS_EPS = 1e-6

GLA_HEADS = 4
GLA_DK = D_MODEL // 2
GLA_DV = D_MODEL
GLA_DK_HEAD = GLA_DK // GLA_HEADS
GLA_DV_HEAD = GLA_DV // GLA_HEADS
GLA_GATE_RANK = 16
GLA_GATE_TEMP = 16.0
GLA_CHUNK = 64
GLA_IN_COLS = 2 * GLA_DK + 2 * GLA_DV + GLA_GATE_RANK

LRU_WIDTH = D_MODEL
LRU_BLOCKS = 4
LRU_BLOCK_W = LRU_WIDTH // LRU_BLOCKS
LRU_CONV_W = 4
LRU_C = 8.0

MOE_GROUPS = 4
MOE_EXPERTS_PER_GROUP = 8
MOE_EXPERTS = MOE_GROUPS * MOE_EXPERTS_PER_GROUP
MOE_TOPK = 2
MOE_FF = D_MODEL // 4
MOE_BLOCK = 128

N_GLA_LAYERS = (DEPTH + 1) // 2
N_LRU_LAYERS = DEPTH // 2

kernel_name = "hybrid_gla_rglru_hier_moe"

def rmsnorm(x, w):
    xf = x.astype(jnp.float32)
    y = xf * lax.rsqrt(jnp.mean(xf * xf, axis=-1, keepdims=True) + RMS_EPS)
    return (y * w.astype(jnp.float32)).astype(x.dtype)

def gla_mixer(x, norm_w, w_in, w_alpha, b_alpha, head_norm_w, w_out):
    bsz, seq, _ = x.shape
    n_chunks = seq // GLA_CHUNK
    h = rmsnorm(x, norm_w)
    proj = h @ w_in
    q, k, v, g, lr = jnp.split(
        proj, [GLA_DK, 2 * GLA_DK, 2 * GLA_DK + GLA_DV, 2 * GLA_DK + 2 * GLA_DV], axis=-1)
    log_a = jax.nn.log_sigmoid((lr @ w_alpha + b_alpha).astype(jnp.float32)) / GLA_GATE_TEMP

    def to_chunks(t, d):
        t = t.reshape(bsz, n_chunks, GLA_CHUNK, GLA_HEADS, d)
        return t.transpose(0, 3, 1, 2, 4).astype(jnp.float32)

    q = to_chunks(q, GLA_DK_HEAD) * (GLA_DK_HEAD ** -0.5)
    k = to_chunks(k, GLA_DK_HEAD)
    v = to_chunks(v, GLA_DV_HEAD)
    la = to_chunks(log_a, GLA_DK_HEAD)
    cum = jnp.cumsum(la, axis=3)
    ref = cum[:, :, :, GLA_CHUNK // 2:GLA_CHUNK // 2 + 1]

    q_in = q * jnp.exp(cum - ref)
    k_in = k * jnp.exp(ref - cum)
    causal = jnp.tril(jnp.ones((GLA_CHUNK, GLA_CHUNK), dtype=bool))
    scores = jnp.einsum('bhncd,bhnsd->bhncs', q_in, k_in)
    scores = jnp.where(causal, scores, 0.0)
    o_intra = jnp.einsum('bhncs,bhnse->bhnce', scores, v)

    last = cum[:, :, :, -1]
    k_st = k * jnp.exp(last[:, :, :, None, :] - cum)
    u = jnp.einsum('bhncd,bhnce->bhnde', k_st, v)

    def step(state, inp):
        decay, u_n = inp
        return decay[..., None] * state + u_n, state

    state0 = jnp.zeros((bsz, GLA_HEADS, GLA_DK_HEAD, GLA_DV_HEAD), jnp.float32)
    _, s_prev = lax.scan(step, state0, (jnp.moveaxis(jnp.exp(last), 2, 0), jnp.moveaxis(u, 2, 0)))
    s_prev = jnp.moveaxis(s_prev, 0, 2)
    o_inter = jnp.einsum('bhncd,bhnde->bhnce', q * jnp.exp(cum), s_prev)

    o = (o_intra + o_inter).transpose(0, 2, 3, 1, 4).reshape(bsz, seq, GLA_HEADS, GLA_DV_HEAD)
    o = rmsnorm(o, head_norm_w)
    o = o.reshape(bsz, seq, GLA_DV) * jax.nn.silu(g.astype(jnp.float32))
    return o.astype(x.dtype) @ w_out

def _lru_combine(left, right):
    a_l, b_l = left
    a_r, b_r = right
    return a_l * a_r, a_r * b_l + b_r

def rglru_mixer(x, norm_w, w_in, conv_w, conv_b, w_rgate, b_rgate, w_igate, b_igate, lam, w_out):
    bsz, seq, _ = x.shape
    h = rmsnorm(x, norm_w)
    xb, gb = jnp.split(h @ w_in, 2, axis=-1)
    gate = jax.nn.gelu(gb, approximate=True)
    xp = jnp.pad(xb, ((0, 0), (LRU_CONV_W - 1, 0), (0, 0)))
    xc = conv_b + xp[:, 0:seq] * conv_w[0]
    for tap in range(1, LRU_CONV_W):
        xc = xc + xp[:, tap:tap + seq] * conv_w[tap]
    xr = xc.reshape(bsz, seq, LRU_BLOCKS, LRU_BLOCK_W)
    r = jax.nn.sigmoid(jnp.einsum('bsni,nij->bsnj', xr, w_rgate).reshape(bsz, seq, LRU_WIDTH) + b_rgate)
    i = jax.nn.sigmoid(jnp.einsum('bsni,nij->bsnj', xr, w_igate).reshape(bsz, seq, LRU_WIDTH) + b_igate)
    log_a = -LRU_C * r.astype(jnp.float32) * jax.nn.softplus(-lam.astype(jnp.float32))
    a = jnp.exp(log_a)
    mult = jnp.sqrt(-jnp.expm1(2.0 * log_a))
    xn = xc.astype(jnp.float32) * i.astype(jnp.float32) * mult
    _, hs = lax.associative_scan(_lru_combine, (a, xn), axis=1)
    y = hs.astype(x.dtype) * gate
    return y @ w_out

def hier_moe(x, norm_w, w_group, w_expert, w_gate, w_up, w_down):
    bsz, seq, d = x.shape
    n_tok = bsz * seq
    h = rmsnorm(x, norm_w).reshape(n_tok, d)
    grp_logits = (h @ w_group).astype(jnp.float32)
    grp_prob = jax.nn.softmax(grp_logits, axis=-1)
    g_sel = jnp.argmax(grp_logits, axis=-1)
    p_g = jnp.take_along_axis(grp_prob, g_sel[:, None], axis=-1)[:, 0]
    exp_logits = (h @ w_expert).astype(jnp.float32).reshape(n_tok, MOE_GROUPS, MOE_EXPERTS_PER_GROUP)
    exp_logits = jnp.take_along_axis(exp_logits, g_sel[:, None, None], axis=1)[:, 0]
    exp_prob = jax.nn.softmax(exp_logits, axis=-1)
    top_p, top_e = lax.top_k(exp_prob, MOE_TOPK)
    top_p = top_p / jnp.sum(top_p, axis=-1, keepdims=True)
    weights = p_g[:, None] * top_p
    eid = g_sel[:, None] * MOE_EXPERTS_PER_GROUP + top_e

    n_assign = n_tok * MOE_TOPK
    eid_f = eid.reshape(-1).astype(jnp.int32)
    w_f = weights.reshape(-1)
    tok_f = jnp.repeat(jnp.arange(n_tok, dtype=jnp.int32), MOE_TOPK)
    order = jnp.argsort(eid_f)
    s_eid, s_tok, s_w = eid_f[order], tok_f[order], w_f[order]
    counts = jnp.bincount(eid_f, length=MOE_EXPERTS)
    starts = jnp.cumsum(counts) - counts
    pcounts = ((counts + MOE_BLOCK - 1) // MOE_BLOCK) * MOE_BLOCK
    pends = jnp.cumsum(pcounts)
    pstarts = pends - pcounts
    dest = pstarts[s_eid] + (jnp.arange(n_assign, dtype=jnp.int32) - starts[s_eid])
    n_blocks = (n_assign + MOE_BLOCK - 1) // MOE_BLOCK + MOE_EXPERTS
    n_rows = n_blocks * MOE_BLOCK
    buf_tok = jnp.full((n_rows,), n_tok, jnp.int32).at[dest].set(s_tok)
    buf_w = jnp.zeros((n_rows,), jnp.float32).at[dest].set(s_w)
    blk_start = jnp.arange(n_blocks, dtype=jnp.int32) * MOE_BLOCK
    blk_eid = jnp.minimum(jnp.searchsorted(pends, blk_start, side='right'), MOE_EXPERTS - 1)
    h_pad = jnp.concatenate([h, jnp.zeros((1, d), h.dtype)], axis=0)
    xb = h_pad[buf_tok].reshape(n_blocks, MOE_BLOCK, d)

    def expert_block(args):
        xblk, e = args
        return (jax.nn.silu(xblk @ w_gate[e]) * (xblk @ w_up[e])) @ w_down[e]

    yb = lax.map(expert_block, (xb, blk_eid)).reshape(n_rows, d)
    yb = yb * buf_w[:, None].astype(yb.dtype)
    out = jnp.zeros((n_tok + 1, d), yb.dtype).at[buf_tok].add(yb)[:n_tok]
    return out.reshape(bsz, seq, d).astype(x.dtype)

def setup_inputs(seed: int = 0) -> dict:
    key = jax.random.key(seed)
    ks = jax.random.split(key, 32)
    f32 = jnp.float32

    def nrm(k, shape, fan_in):
        return jax.random.normal(k, shape, f32) * (fan_in ** -0.5)

    def gain(k, shape):
        return 1.0 + 0.02 * jax.random.normal(k, shape, f32)

    def small(k, shape, s=0.02):
        return s * jax.random.normal(k, shape, f32)

    ng, nl, L = N_GLA_LAYERS, N_LRU_LAYERS, DEPTH
    u = jax.random.uniform(ks[18], (nl, LRU_WIDTH), f32, minval=0.9, maxval=0.999)
    s = u ** (1.0 / LRU_C)
    lam = jnp.log(s) - jnp.log1p(-s)
    return {
        "x": jax.random.normal(ks[0], (BATCH, SEQ, D_MODEL), f32),
        "gla_norm": gain(ks[1], (ng, D_MODEL)),
        "gla_w_in": nrm(ks[2], (ng, D_MODEL, GLA_IN_COLS), D_MODEL),
        "gla_w_alpha": nrm(ks[3], (ng, GLA_GATE_RANK, GLA_DK), GLA_GATE_RANK),
        "gla_b_alpha": small(ks[4], (ng, GLA_DK), 0.1),
        "gla_head_norm": gain(ks[5], (ng, GLA_DV_HEAD)),
        "gla_w_out": nrm(ks[6], (ng, GLA_DV, D_MODEL), GLA_DV),
        "lru_norm": gain(ks[7], (nl, D_MODEL)),
        "lru_w_in": nrm(ks[8], (nl, D_MODEL, 2 * LRU_WIDTH), D_MODEL),
        "lru_conv_w": nrm(ks[9], (nl, LRU_CONV_W, LRU_WIDTH), LRU_CONV_W),
        "lru_conv_b": small(ks[10], (nl, LRU_WIDTH)),
        "lru_w_rgate": nrm(ks[11], (nl, LRU_BLOCKS, LRU_BLOCK_W, LRU_BLOCK_W), LRU_BLOCK_W),
        "lru_b_rgate": small(ks[12], (nl, LRU_WIDTH)),
        "lru_w_igate": nrm(ks[13], (nl, LRU_BLOCKS, LRU_BLOCK_W, LRU_BLOCK_W), LRU_BLOCK_W),
        "lru_b_igate": small(ks[14], (nl, LRU_WIDTH)),
        "lru_lambda": lam,
        "lru_w_out": nrm(ks[15], (nl, LRU_WIDTH, D_MODEL), LRU_WIDTH),
        "moe_norm": gain(ks[16], (L, D_MODEL)),
        "moe_w_group": nrm(ks[17], (L, D_MODEL, MOE_GROUPS), D_MODEL),
        "moe_w_expert": nrm(ks[19], (L, D_MODEL, MOE_EXPERTS), D_MODEL),
        "moe_w_gate": nrm(ks[20], (L, MOE_EXPERTS, D_MODEL, MOE_FF), D_MODEL),
        "moe_w_up": nrm(ks[21], (L, MOE_EXPERTS, D_MODEL, MOE_FF), D_MODEL),
        "moe_w_down": nrm(ks[22], (L, MOE_EXPERTS, MOE_FF, D_MODEL), MOE_FF),
        "final_norm": gain(ks[23], (D_MODEL,)),
    }

def reference(x, gla_norm, gla_w_in, gla_w_alpha, gla_b_alpha, gla_head_norm, gla_w_out,
              lru_norm, lru_w_in, lru_conv_w, lru_conv_b, lru_w_rgate, lru_b_rgate,
              lru_w_igate, lru_b_igate, lru_lambda, lru_w_out,
              moe_norm, moe_w_group, moe_w_expert, moe_w_gate, moe_w_up, moe_w_down,
              final_norm):
    for layer in range(DEPTH):
        j = layer // N_MIXERS
        if layer % N_MIXERS == 0:
            x = x + gla_mixer(x, gla_norm[j], gla_w_in[j], gla_w_alpha[j], gla_b_alpha[j],
                              gla_head_norm[j], gla_w_out[j])
        else:
            x = x + rglru_mixer(x, lru_norm[j], lru_w_in[j], lru_conv_w[j], lru_conv_b[j],
                                lru_w_rgate[j], lru_b_rgate[j], lru_w_igate[j], lru_b_igate[j],
                                lru_lambda[j], lru_w_out[j])
        x = x + hier_moe(x, moe_norm[layer], moe_w_group[layer], moe_w_expert[layer],
                         moe_w_gate[layer], moe_w_up[layer], moe_w_down[layer])
    return rmsnorm(x, final_norm)


_drawn_inputs = setup_inputs


def setup_inputs(seed=0):
    import zlib

    import numpy as np

    out = dict(_drawn_inputs(seed))
    spreads = {}
    factors = {'lru_norm': 3.126, 'lru_b_rgate': 8.0, 'lru_b_igate': 6.071, 'final_norm': 2.905}
    for name, (base, spread) in spreads.items():
        noise = np.random.default_rng([zlib.crc32(name.encode()), seed]).standard_normal(out[name].shape)
        drawn = base * np.exp(spread * noise) if base else spread * noise
        out[name] = jnp.asarray(drawn.astype(out[name].dtype))
    for name, factor in factors.items():
        out[name] = (out[name] * factor).astype(out[name].dtype)
    return out
```

```python
import math
from contextlib import ExitStack

import concourse.bass as bass
from concourse import mybir
from concourse.alu_op_type import AluOpType as ALU

ACT = mybir.ActivationFunctionType
AX = mybir.AxisListType
F32 = mybir.dt.float32
F32R = mybir.dt.float32r
BF16 = mybir.dt.bfloat16
I32 = mybir.dt.int32
U32 = mybir.dt.uint32

P = 128
BANK = 512
START = 2
DMA = 16

T = 2048
D = 1024
KD = D // P
NT = T // P
EPS = 1e-6

HALVES = 2
TH = T // HALVES
HT = TH // P
GROUP = 512
NG = TH // GROUP
GT = GROUP // P

HEADS = 4
DK = 128
DV = 256
RANK = 16
CHUNK = 64
NC = GROUP // CHUNK
GATE_TEMP = 16.0

LRU_BLOCKS = 4
LBW = 256
LCT = LBW // P
TAPS = 4
LRU_STEPS = 33
LRU_C = 8.0

GROUPS = 4
EPG = 8
E = GROUPS * EPG
FF = 256
KF = FF // P
SLOTS = T // P
MAX_BLOCKS = 2 * T // P + E
MIN_BLOCKS = E


def nth(k):
    return k + (START + 1)


def nth_dma(k):
    return k * DMA + DMA


def nth_store(k):
    return k * DMA + DMA * (START + 1)


class Steps:

    def __init__(self, eng, sem):
        self.eng, self.sem, self.base, self.n = eng, sem, 0, 0

    def __call__(self, ins):
        self.add(ins)
        self.wait()

    def add(self, ins):
        ins.then_inc(self.sem, 1)
        self.n += 1

    def wait(self):
        self.eng.wait_ge(self.sem, self.base + self.n)

    def loop(self, done):
        self.base, self.n = done, 0

    def after(self, done):
        self.base, self.n = done, 0


def matmul3(nc, out, w_hi, w_lo, x_hi, x_lo, first, last):
    nc.tensor.matmul(out, w_hi, x_hi, start=first, stop=False)
    nc.tensor.matmul(out, w_hi, x_lo, start=False, stop=False)
    return nc.tensor.matmul(out, w_lo, x_hi, start=False, stop=last)


class Memory:

    def __init__(self, nc, ctx, stage):
        self.nc, self.ctx, self.stage = nc, ctx, stage
        self.primed, self.stores, self.held = [], [], []

    def sb(self, name, shape, dt=F32):
        return self.ctx.enter_context(self.nc.sbuf_tensor(f"{self.stage}_{name}", shape, dt))

    def ps(self, name, shape, dt=F32):
        return self.ctx.enter_context(self.nc.psum_tensor(f"{self.stage}_{name}", shape, dt))

    def plain(self, name):
        s = self.nc.alloc_semaphore(name=f"{self.stage}_{name}")
        self.held.append(s)
        return s

    def sem(self, name):
        s = self.plain(name)
        self.primed.append(s)
        return s

    def store(self, name):
        s = self.plain(name)
        self.stores.append(s)
        return s

    def block(self):
        self.block_ctx = ExitStack()
        return self.block_ctx.enter_context(self.nc.Block())

    def end(self):
        self.block_ctx.close()
        self.nc.clear_and_free_semaphores(self.held)
        self.nc.all_engine_barrier()

    def prime(self, sp):
        for s in self.primed:
            sp.sem_inc(s, START)
        for s in self.stores:
            sp.sem_inc(s, START * DMA)


def stand(eng):
    eng.nop(nofuse=True)


class Consts:

    def __init__(self, nc, ctx):
        def sb(name, shape, dt=F32):
            return ctx.enter_context(nc.sbuf_tensor(name, shape, dt))

        self.ident = sb("ident", [P, P])
        self.causal = sb("causal", [P, P])
        self.keep = sb("keep", [P, GROUP])
        self.before = sb("before", [P, P], BF16)
        self.ones_bf = sb("ones_bf", [P, P], BF16)
        self.ones_row = sb("ones_row", [P, E])
        self.token = sb("token", [P, NT], I32)
        self.expert_no = sb("expert_no", [P, E])
        self.last_first = sb("last_first", [P, EPG])
        self.eps = sb("eps", [P, 1])
        self.weight = sb("weight", [P, NT, 2])
        self.row = sb("row", [P, NT, 2], I32)
        self.blocks = sb("blocks", [P, E], I32)
        self.block_at = sb("block_at", [P, E], I32)


def constants(nc, k):
    with ExitStack() as ctx:
        made = ctx.enter_context(nc.semaphore("constants_made"))
        block = ctx.enter_context(nc.Block())

        @block.gpsimd
        def _(pool):
            done = Steps(pool, made)
            done.add(pool.memset(k.ident[:], 0.0))
            done.add(pool.memset(k.causal[:], 1.0))
            done.add(pool.memset(k.keep[:], 1.0))
            done.add(pool.memset(k.before[:], 1.0))
            done.add(pool.memset(k.ones_bf[:], 1.0))
            done.add(pool.memset(k.ones_row[:], 1.0))
            done.add(pool.memset(k.eps[:], EPS))
            done.add(pool.iota(k.token[:], [[P, NT]], base=0, channel_multiplier=1))
            done.add(pool.iota(k.expert_no[:], [[1, E]], base=0, channel_multiplier=0,
                               allow_small_or_imprecise_dtypes=True))
            done.add(pool.iota(k.last_first[:], [[-1, EPG]], base=EPG, channel_multiplier=0,
                               allow_small_or_imprecise_dtypes=True))
            done.wait()
            done.add(pool.affine_select(out=k.ident[:], in_=k.ident[:], compare_op=ALU.not_equal,
                                        fill=1.0, base=0, pattern=[[-1, P]], channel_multiplier=1))
            done.add(pool.affine_select(out=k.causal[:], in_=k.causal[:], compare_op=ALU.is_ge,
                                        fill=0.0, base=0, pattern=[[1, P]], channel_multiplier=-1))
            done.add(pool.affine_select(out=k.before[:], in_=k.before[:], compare_op=ALU.is_gt,
                                        fill=0.0, base=0, pattern=[[1, P]], channel_multiplier=-1))
            chunk_starts = k.keep[:].rearrange("p (c t) -> p c t", t=CHUNK)[:, :, 0]
            done.add(pool.memset(chunk_starts, 0.0))
            done.wait()
            done(pool.memset(k.causal[0:CHUNK, CHUNK:P], 0.0))


class Norm:

    def __init__(self, m, k, x, h, square):
        self.x, self.h, self.eps, self.square = x, h, k.eps, square
        self.norm_w = m.sb("norm_w", [P, D])
        self.ss = m.sb("ss", [P, 2])
        self.std = m.sb("std", [P, 2])
        self.rstd = m.sb("rstd", [P, 2])
        self.norm_w_in = m.plain("norm_w_in")
        self.ss_done = m.sem("ss_done")
        self.std_done = m.sem("std_done")
        self.h_done = m.sem("h_done")

    def scalar(self, nc, act, j, t):
        act.wait_ge(self.std_done, nth(t - 2))
        nc.scalar.activation(self.square, self.x[:, j], ACT.Square, accum_out=self.ss[:, j:j + 1])\
            .then_inc(self.ss_done, 1)
        act.wait_ge(self.h_done, nth(t - 2))
        act.wait_ge(self.ss_done, nth(t))
        nc.scalar.activation(self.std[:, j:j + 1], self.ss[:, j:j + 1], ACT.Sqrt,
                             bias=self.eps[:, 0:1], scale=1.0 / D).then_inc(self.std_done, 1)

    def vector(self, nc, dve, step, j, t):
        dve.wait_ge(self.std_done, nth(t))
        step(nc.vector.reciprocal(self.rstd[:, j:j + 1], self.std[:, j:j + 1]))
        nc.vector.scalar_tensor_tensor(out=self.h[:, j], in0=self.x[:, j], scalar=self.rstd[:, j:j + 1],
                                       in1=self.norm_w[:], op0=ALU.mult, op1=ALU.mult)\
            .then_inc(self.h_done, 1)


def gla(nc, k, x_dram, norm_w, w_in, w_alpha, b_alpha, head_norm, oT_dram):
    with ExitStack() as ctx:
        m = Memory(nc, ctx, "gla")
        hT_hi = m.sb("hT_hi", [P, KD, TH], F32R)
        hT_lo = m.sb("hT_lo", [P, KD, TH], F32R)
        work = m.sb("work", [P, 4, D])
        q_k = m.sb("q_k", [P, 2 * GROUP])
        q_sb, k_sb = q_k[:, 0:GROUP], q_k[:, GROUP:]
        norm = Norm(m, k, work[:, 0:2], work[:, 2:4], q_k[:, 0:D])
        vg = work[:, 0:2].rearrange("p a (b c) -> p (a b) c", c=2 * DV)
        o_raw = work[:, 2].rearrange("p (a c) -> p a c", c=DV)
        gated = work[:, 3].rearrange("p (a c) -> p a c", c=DV)

        w_raw = m.sb("w_raw", [P, KD * 2 * DV])
        wqk_raw = w_raw[:, 0:KD * 2 * DK].rearrange("p (k c) -> p k c", k=KD)
        wvg_raw = w_raw[:].rearrange("p (k c) -> p k c", k=KD)
        wqk_hi = m.sb("wqk_hi", [P, KD, 2 * DK], F32R)
        wqk_lo = m.sb("wqk_lo", [P, KD, 2 * DK], F32R)
        wvg_hi = m.sb("wvg_hi", [P, KD, 2 * DV], F32R)
        wvg_lo = m.sb("wvg_lo", [P, KD, 2 * DV], F32R)
        wlr_raw = m.sb("wlr_raw", [P, KD, RANK])
        wlr_hi = m.sb("wlr_hi", [P, KD, RANK], F32R)
        wlr_lo = m.sb("wlr_lo", [P, KD, RANK], F32R)
        wal_in, wal = m.sb("w_alpha_in", [RANK, DK]), m.sb("w_alpha", [RANK, DK])
        bal_in, bal = m.sb("b_alpha_in", [P, 1]), m.sb("b_alpha", [P, 1])
        hn = m.sb("head_norm", [P, DV // P])
        lrT = m.sb("lrT", [RANK, TH])

        q_in, k_in, q_x, k_x, q_dec, k_dec = (m.sb(s, [P, NG, GROUP]) for s in (
            "q_in", "k_in", "q_x", "k_x", "q_dec", "k_dec"))
        tile_decay = m.sb("tile_decay", [P, NG, GT])
        z = m.sb("z", [P, GROUP])
        soft = m.sb("soft", [P, GROUP])
        cum = m.sb("cum", [P, GROUP])
        to_mid = soft
        to_end = m.sb("to_end", [P, GROUP])
        e_chunk = m.sb("e_chunk", [P, NC])
        state = m.sb("state", [P, HEADS, DV])
        o_square = m.sb("o_square", [P, DV])
        sT = m.sb("sT", [P, P])
        kd = m.sb("kd", [P, P])
        oss = m.sb("oss", [P, GT])
        ostd = m.sb("ostd", [P, GT])
        orstd = m.sb("orstd", [P, GT])
        oT = m.sb("oT", [P, DV // P, GROUP])

        ps = m.ps("ps", [P, 8, BANK])
        Q, K, LA, VG, SC, O, UP = 0, 1, 2, 3, 5, 6, 7

        x_in = [m.plain(f"x_in{j}") for j in range(2)]
        hT_ps_done, hT_hi_done, hT_lo_done = m.sem("hT_ps_done"), m.sem("hT_hi_done"), m.sem("hT_lo_done")
        small_in = m.plain("small_in")
        wlr_done, zeroed = m.plain("wlr_done"), m.plain("zeroed")
        wqk_in, wvg_in = m.plain("wqk_in"), m.plain("wvg_in")
        wqk_hi_done, wqk_lo_done = m.sem("wqk_hi_done"), m.sem("wqk_lo_done")
        wvg_hi_done, wvg_lo_done = m.sem("wvg_hi_done"), m.sem("wvg_lo_done")
        lr_ps_done, lrT_done = m.sem("lr_ps_done"), m.sem("lrT_done")
        qkz_ps_done = m.sem("qkz_ps_done")
        soft_steps = m.sem("soft_steps")
        cum_done, exps_done, group_done = m.sem("cum_done"), m.sem("exps_done"), m.sem("group_done")
        vg_ps_done, vg_done = m.sem("vg_ps_done"), m.sem("vg_done")
        sc_ps_done, sc_done = m.sem("sc_ps_done"), m.sem("sc_done")
        ou_ps_done = m.sem("ou_ps_done")
        o_raw_done, state_done = m.sem("o_raw_done"), m.sem("state_done")
        oss_done, ostd_done = m.sem("oss_done"), m.sem("ostd_done")
        og_done, oT_ps_done, oT_done = m.sem("og_done"), m.sem("oT_ps_done"), m.sem("oT_done")
        oT_stored = m.store("oT_stored")
        order = m.plain("vector_order")
        block = m.block()

        w_rows = w_in.rearrange("(k p) c -> p k c", p=P)
        KC, VC = HEADS * DK, 2 * HEADS * DK
        GC, LC = VC + D, VC + 2 * D

        @block.sync
        def _(sp):
            m.prime(sp)

            def load_qk(h):
                sp.dma_start(wqk_raw[:, :, 0:DK], w_rows[:, :, bass.ds(h * DK, DK)]).then_inc(wqk_in, DMA)
                sp.dma_start(wqk_raw[:, :, DK:], w_rows[:, :, bass.ds(h * DK + KC, DK)]).then_inc(wqk_in, DMA)
                sp.dma_start(wal_in[:], w_alpha[:, bass.ds(h * DK, DK)]).then_inc(wqk_in, DMA)
                with nc.allow_non_contiguous_dma(reason="128 biases"):
                    sp.dma_start(bal_in[:], b_alpha.rearrange("(c o) -> c o", o=1)[bass.ds(h * DK, DK), :])\
                        .then_inc(wqk_in, DMA)

            def load_vg(h):
                sp.dma_start(wvg_raw[:, :, 0:DV], w_rows[:, :, bass.ds(h * DV + VC, DV)]).then_inc(wvg_in, DMA)
                sp.dma_start(wvg_raw[:, :, DV:], w_rows[:, :, bass.ds(h * DV + GC, DV)]).then_inc(wvg_in, DMA)

            sp.dma_start(norm.norm_w[:], norm_w.partition_broadcast(P)).then_inc(norm.norm_w_in, DMA)
            for i in range(2):
                sp.dma_start(norm.x[:, i], x_dram[i * P:(i + 1) * P, :]).then_inc(x_in[i], DMA)
            sp.dma_start(wlr_raw[:], w_rows[:, :, LC:LC + RANK]).then_inc(small_in, DMA)
            with nc.allow_non_contiguous_dma(reason="256 gains"):
                sp.dma_start(hn[:], head_norm.rearrange("(h p) -> p h", p=P)).then_inc(small_in, DMA)
            load_qk(0)
            sp.wait_ge(wqk_lo_done, nth(0))
            load_vg(0)
            with sp.Fori(0, HALVES) as half:
                for i in range(2, HT):
                    sp.wait_ge(norm.h_done, nth(half * HT + (i - 2)))
                    sp.dma_start(norm.x[:, i % 2], x_dram[bass.ds(half * TH + i * P, P), :])\
                        .then_inc(x_in[i % 2], DMA)
                with sp.Fori(0, HEADS) as h:
                    n = half * HEADS + h
                    sp.wait_ge(wvg_lo_done, nth(n))
                    load_qk((h + 1) % HEADS)
                    sp.wait_ge(wqk_lo_done, nth(n + 1))
                    load_vg((h + 1) % HEADS)
                    for g in range(NG):
                        sp.wait_ge(oT_done, nth(n * NG + g))
                        for e in range(DV // P):
                            sp.dma_start(oT_dram[bass.ds(h * DV + e * P, P),
                                                 bass.ds(half * TH + g * GROUP, GROUP)],
                                         oT[:, e]).then_inc(oT_stored, DMA)
                for i in range(2):
                    sp.dma_start(norm.x[:, i], x_dram[bass.ds(((half + 1) % HALVES) * TH + i * P, P), :])\
                        .then_inc(x_in[i], DMA)
            sp.wait_ge(oT_stored, nth_store(HALVES * HEADS * NG * (DV // P) - 1))
            sp.wait_ge(wqk_in, nth_dma(4 * HALVES * HEADS + 3))
            sp.wait_ge(wvg_in, nth_dma(2 * HALVES * HEADS + 1))
            for i in range(2):
                sp.wait_ge(x_in[i], nth_dma(HALVES * HT // 2))

        @block.scalar
        def _(act):
            def split_qk(n):
                act.wait_ge(wqk_in, nth_dma(4 * n + 3))
                nc.scalar.activation(wqk_hi[:], wqk_raw, ACT.Copy).then_inc(wqk_hi_done, 1)

            def square_o(i, t):
                act.wait_ge(oss_done, nth(t - 1))
                act.wait_ge(o_raw_done, nth(t))
                nc.scalar.activation(o_square[:], o_raw[:, i], ACT.Square,
                                     accum_out=oss[:, i:i + 1]).then_inc(oss_done, 1)

            def take_oT(ng):
                act.wait_ge(oT_ps_done, nth(ng))
                act.wait_ge(oT_stored, nth_store(2 * ng - 1))
                for e in range(DV // P):
                    last = nc.scalar.activation(oT[:, e], ps[:, Q + e], ACT.Copy, scale=hn[:, e:e + 1])
                last.then_inc(oT_done, 1)

            act.wait_ge(small_in, nth_dma(1))
            nc.scalar.activation(wlr_hi[:], wlr_raw[:], ACT.Copy).then_inc(wlr_done, 1)
            split_qk(0)
            with act.Fori(0, HALVES) as half:
                for i in range(HT):
                    t = half * HT + i
                    act.wait_ge(x_in[i % 2], nth_dma(half * (HT // 2) + i // 2))
                    norm.scalar(nc, act, i % 2, t)
                    act.wait_ge(hT_ps_done, nth(t))
                    for b in range(2):
                        nc.scalar.activation(hT_hi[:, 4 * b:4 * b + 4, i * P:(i + 1) * P],
                                             ps[:, 2 * (i % 2) + b].rearrange("p (a c) -> p a c", c=P),
                                             ACT.Copy).then_inc(hT_hi_done, 1)
                for g in range(NG):
                    act.wait_ge(lr_ps_done, nth(half * NG + g))
                    nc.scalar.activation(lrT[:, g * GROUP:(g + 1) * GROUP], ps[0:RANK, LA], ACT.Copy)\
                        .then_inc(lrT_done, 1)
                with act.Fori(0, HEADS) as h:
                    n = half * HEADS + h
                    act.wait_ge(wvg_in, nth_dma(2 * n + 1))
                    act.wait_ge(vg_ps_done, nth(n * HT - 1))
                    nc.scalar.activation(wvg_hi[:], wvg_raw, ACT.Copy).then_inc(wvg_hi_done, 1)
                    for g in range(NG):
                        ng = n * NG + g
                        act.wait_ge(group_done, nth(ng - 1))
                        act.wait_ge(qkz_ps_done, nth(3 * ng))
                        nc.scalar.activation(q_sb, ps[:, Q], ACT.Copy, scale=DK ** -0.5)
                        act.wait_ge(qkz_ps_done, nth(3 * ng + 1))
                        nc.scalar.activation(k_sb, ps[:, K], ACT.Copy)
                        act.wait_ge(qkz_ps_done, nth(3 * ng + 2))
                        nc.scalar.activation(z[:], ps[:, LA], ACT.Identity, bias=bal[:])\
                            .then_inc(soft_steps, 1)
                        act.wait_ge(soft_steps, nth(4 * ng))
                        nc.scalar.activation(soft[:], z[:], ACT.Abs).then_inc(soft_steps, 1)
                        act.wait_ge(soft_steps, nth(4 * ng + 1))
                        nc.scalar.activation(soft[:], soft[:], ACT.Exp, scale=-1.0).then_inc(soft_steps, 1)
                        act.wait_ge(soft_steps, nth(4 * ng + 2))
                        nc.scalar.activation(soft[:], soft[:], ACT.Ln, bias=1.0).then_inc(soft_steps, 1)
                        act.wait_ge(cum_done, nth(ng))
                        s = 1.0 / GATE_TEMP
                        chunk_ends = cum[:].rearrange("p (c t) -> p c t", t=CHUNK)[:, :, CHUNK - 1]
                        nc.scalar.activation(q_in[:, g], to_mid[:], ACT.Exp, scale=s)
                        nc.scalar.activation(k_in[:, g], to_mid[:], ACT.Exp, scale=-s)
                        nc.scalar.activation(k_x[:, g], to_end[:], ACT.Exp, scale=s)
                        nc.scalar.activation(q_x[:, g], cum[:], ACT.Exp, scale=s)
                        nc.scalar.activation(e_chunk[:], chunk_ends, ACT.Exp, scale=s).then_inc(exps_done, 1)
                    split_qk(n + 1)
                    for g in range(NG):
                        ng = n * NG + g
                        for i in range(GT):
                            t = n * HT + g * GT + i
                            if i == 0:
                                act.wait_ge(ostd_done, nth(ng - 1))
                            act.wait_ge(vg_ps_done, nth(t))
                            nc.scalar.activation(vg[:, i], ps[:, VG + i % 2], ACT.Copy).then_inc(vg_done, 1)
                            if i:
                                square_o(i - 1, t - 1)
                            if g and i == 2:
                                take_oT(ng - 1)
                        square_o(GT - 1, t)
                        nc.scalar.activation(gated, vg[:, :, DV:], ACT.Silu)
                        act.wait_ge(oss_done, nth(t))
                        nc.scalar.activation(ostd[:], oss[:], ACT.Sqrt, bias=k.eps[:, 0:1], scale=1.0 / DV)\
                            .then_inc(ostd_done, 1)
                    take_oT(n * NG + NG - 1)

        STEPS_PER_HEAD = 12
        STEPS_PER_HALF = HT + HEADS * STEPS_PER_HEAD

        @block.vector
        def _(dve):
            step = Steps(dve, order)
            nc.vector.memset(sT[:], 0.0)
            nc.vector.memset(state[:], 0.0).then_inc(zeroed, 1)
            dve.wait_ge(zeroed, 1)
            dve.wait_ge(wlr_done, 1)
            nc.vector.tensor_tensor(wlr_lo[:], wlr_raw[:], wlr_hi[:].bitcast(F32), ALU.subtract)\
                .then_inc(wlr_done, 1)
            dve.wait_ge(norm.norm_w_in, nth_dma(0))

            def split_qk(n):
                dve.wait_ge(wqk_hi_done, nth(n))
                nc.vector.tensor_copy(wal[:], wal_in[:])
                nc.vector.tensor_copy(bal[:], bal_in[:])
                nc.vector.tensor_tensor(wqk_lo[:], wqk_raw, wqk_hi[:].bitcast(F32), ALU.subtract)\
                    .then_inc(wqk_lo_done, 1)

            def chunks(x):
                return x.rearrange("p (c t) -> p c t", t=CHUNK)

            def two_chunks(x):
                return x.rearrange("p (a b t) -> p a b t", b=2, t=CHUNK)

            split_qk(0)
            with dve.Fori(0, HALVES) as half:
                step.loop(half * STEPS_PER_HALF)
                for i in range(HT):
                    t = half * HT + i
                    dve.wait_ge(hT_ps_done, nth(t - 2))
                    norm.vector(nc, dve, step, i % 2, t)
                    for b in range(2):
                        dve.wait_ge(hT_hi_done, nth(2 * t + b))
                        part = (slice(None), slice(4 * b, 4 * b + 4), slice(i * P, (i + 1) * P))
                        last = nc.vector.tensor_tensor(
                            hT_lo[part], ps[:, 2 * (i % 2) + b].rearrange("p (a c) -> p a c", c=P),
                            hT_hi[part].bitcast(F32), ALU.subtract)
                    last.then_inc(hT_lo_done, 1)
                with dve.Fori(0, HEADS) as h:
                    n = half * HEADS + h
                    step.loop(half * STEPS_PER_HALF + h * STEPS_PER_HEAD + HT)
                    dve.wait_ge(wvg_hi_done, nth(n))
                    nc.vector.tensor_tensor(wvg_lo[:], wvg_raw, wvg_hi[:].bitcast(F32), ALU.subtract)\
                        .then_inc(wvg_lo_done, 1)
                    for g in range(NG):
                        ng = n * NG + g
                        dve.wait_ge(soft_steps, nth(4 * ng + 3))
                        step(nc.vector.tensor_scalar(z[:], z[:], 0.0, None, ALU.min))
                        step(nc.vector.tensor_tensor(z[:], z[:], soft[:], ALU.subtract))
                        step(nc.vector.tensor_tensor_scan(cum[:], k.keep[:], z[:], 0.0, ALU.mult, ALU.add))
                        c = chunks(cum[:])
                        mid = c[:, :, CHUNK // 2:CHUNK // 2 + 1].to_broadcast([P, NC, CHUNK])
                        end = c[:, :, CHUNK - 1:CHUNK].to_broadcast([P, NC, CHUNK])
                        nc.vector.tensor_tensor(chunks(to_mid[:]), c, mid, ALU.subtract)
                        nc.vector.tensor_tensor(chunks(to_end[:]), end, c, ALU.subtract).then_inc(cum_done, 1)
                        dve.wait_ge(exps_done, nth(ng))
                        step.add(nc.vector.tensor_tensor(k_x[:, g], k_x[:, g], k_sb, ALU.mult))
                        step.add(nc.vector.tensor_tensor(q_x[:, g], q_x[:, g], q_sb, ALU.mult))
                        nc.vector.tensor_tensor(q_in[:, g], q_in[:, g], q_sb, ALU.mult)
                        nc.vector.tensor_tensor(k_in[:, g], k_in[:, g], k_sb, ALU.mult)
                        step.wait()
                        of_pair = e_chunk[:].rearrange("p (a b) -> p a b", b=2)
                        qx, kx = two_chunks(q_x[:, g]), two_chunks(k_x[:, g])
                        qd, kdec = two_chunks(q_dec[:, g]), two_chunks(k_dec[:, g])
                        nc.vector.tensor_copy(qd[:, :, 0], qx[:, :, 0])
                        nc.vector.tensor_tensor(qd[:, :, 1], qx[:, :, 1],
                                                of_pair[:, :, 0:1].to_broadcast([P, GT, CHUNK]), ALU.mult)
                        nc.vector.tensor_tensor(kdec[:, :, 0], kx[:, :, 0],
                                                of_pair[:, :, 1:2].to_broadcast([P, GT, CHUNK]), ALU.mult)
                        nc.vector.tensor_copy(kdec[:, :, 1], kx[:, :, 1])
                        nc.vector.tensor_tensor(tile_decay[:, g], of_pair[:, :, 0], of_pair[:, :, 1],
                                                ALU.mult).then_inc(group_done, 1)
                    split_qk(n + 1)
                    for g in range(NG):
                        ng = n * NG + g
                        for i in range(GT):
                            t = n * HT + g * GT + i
                            dve.wait_ge(ou_ps_done, nth(2 * t - 1))
                            dve.wait_ge(sc_ps_done, nth(t))
                            nc.vector.tensor_copy(kd[:], ps[:, SC, 192:320])
                            for c in range(2):
                                own = (slice(c * CHUNK, (c + 1) * CHUNK), slice(c * CHUNK, (c + 1) * CHUNK))
                                nc.vector.copy_predicated(sT[own], k.causal[own].bitcast(U32),
                                                          ps[:, SC][own])
                            nc.vector.tensor_copy(sT[0:CHUNK, CHUNK:P], ps[0:CHUNK, SC, P:P + CHUNK])\
                                .then_inc(sc_done, 1)
                            dve.wait_ge(ou_ps_done, nth(2 * t))
                            nc.vector.tensor_copy(o_raw[:, i], ps[:, O, 0:DV]).then_inc(o_raw_done, 1)
                            dve.wait_ge(ou_ps_done, nth(2 * t + 1))
                            nc.vector.scalar_tensor_tensor(
                                out=state[:, bass.ds(h, 1)], in0=state[:, bass.ds(h, 1)],
                                scalar=tile_decay[:, g, i:i + 1], in1=ps[:, UP, 0:DV].unsqueeze(1),
                                op0=ALU.mult, op1=ALU.add).then_inc(state_done, 1)
                        dve.wait_ge(ostd_done, nth(ng))
                        step(nc.vector.reciprocal(orstd[:], ostd[:]))
                        for i in range(GT):
                            last = nc.vector.scalar_tensor_tensor(
                                out=gated[:, i], in0=o_raw[:, i], scalar=orstd[:, i:i + 1],
                                in1=gated[:, i], op0=ALU.mult, op1=ALU.mult)
                        last.then_inc(og_done, 1)
                    assert step.n == STEPS_PER_HEAD, step.n

        @block.tensor
        def _(pe):
            def transposed_outputs(ng):
                pe.wait_ge(og_done, nth(ng))
                pe.wait_ge(oT_done, nth(ng - 1))
                for e in range(DV // P):
                    for i in range(GT):
                        last = nc.tensor.transpose(ps[:, Q + e, i * P:(i + 1) * P],
                                                   gated[:, i, e * P:(e + 1) * P], k.ident[:])
                last.then_inc(oT_ps_done, 1)

            pe.wait_ge(wlr_done, 2)
            pe.wait_ge(zeroed, 1)
            with pe.Fori(0, HALVES) as half:
                pe.wait_ge(oT_done, nth(half * (HEADS * NG) - 1))
                for i in range(HT):
                    t = half * HT + i
                    pe.wait_ge(hT_lo_done, nth(t - 2))
                    pe.wait_ge(norm.h_done, nth(t))
                    for c in range(KD):
                        last = nc.tensor.transpose(ps[:, 2 * (i % 2) + c // 4, (c % 4) * P:(c % 4 + 1) * P],
                                                   norm.h[:, i % 2, c * P:(c + 1) * P], k.ident[:])
                    last.then_inc(hT_ps_done, 1)
                pe.wait_ge(hT_lo_done, nth(half * HT + (HT - 1)))
                for g in range(NG):
                    pe.wait_ge(lrT_done, nth(half * NG + (g - 1)))
                    for c in range(KD):
                        cols = slice(g * GROUP, (g + 1) * GROUP)
                        last = matmul3(nc, ps[0:RANK, LA], wlr_hi[:, c], wlr_lo[:, c],
                                       hT_hi[:, c, cols], hT_lo[:, c, cols], c == 0, c == KD - 1)
                    last.then_inc(lr_ps_done, 1)
                pe.wait_ge(lrT_done, nth(half * NG + (NG - 1)))
                stand(pe)
                with pe.Fori(0, HEADS) as h:
                    n = half * HEADS + h
                    pe.wait_ge(oT_done, nth(n * NG - 1))
                    pe.wait_ge(wqk_lo_done, nth(n))
                    for g in range(NG):
                        ng = n * NG + g
                        cols = slice(g * GROUP, (g + 1) * GROUP)
                        if g:
                            pe.wait_ge(soft_steps, nth(4 * (ng - 1)))
                        for bank, at in ((Q, 0), (K, DK)):
                            for c in range(KD):
                                last = matmul3(nc, ps[:, bank], wqk_hi[:, c, at:at + DK],
                                               wqk_lo[:, c, at:at + DK], hT_hi[:, c, cols],
                                               hT_lo[:, c, cols], c == 0, c == KD - 1)
                            last.then_inc(qkz_ps_done, 1)
                        nc.tensor.matmul(ps[:, LA], wal[:], lrT[:, cols], start=True, stop=True)\
                            .then_inc(qkz_ps_done, 1)
                    pe.wait_ge(wvg_lo_done, nth(n))

                    def tile_outputs(i, t, g):
                        at = slice(i * P, (i + 1) * P)
                        values = vg[:, i, 0:DV]
                        pe.wait_ge(sc_done, nth(t))
                        pe.wait_ge(vg_done, nth(t))
                        pe.wait_ge(o_raw_done, nth(t - 1))
                        pe.wait_ge(state_done, nth(t - 1))
                        nc.tensor.matmul(ps[:, O, 0:DV], sT[:], values, start=True, stop=False)
                        nc.tensor.matmul(ps[:, O, 0:DV], q_dec[:, g, at], state[:, bass.ds(h, 1)],
                                         start=False, stop=True).then_inc(ou_ps_done, 1)
                        nc.tensor.matmul(ps[:, UP, 0:DV], kd[:], values, start=True, stop=True)\
                            .then_inc(ou_ps_done, 1)

                    for g in range(NG):
                        ng = n * NG + g
                        for i in range(GT):
                            t = n * HT + g * GT + i
                            at = slice(i * P, (i + 1) * P)
                            tok = slice(g * GROUP + i * P, g * GROUP + (i + 1) * P)
                            pe.wait_ge(vg_done, nth(t - 2))
                            for c in range(KD):
                                last = matmul3(nc, ps[:, VG + i % 2], hT_hi[:, c, tok], hT_lo[:, c, tok],
                                               wvg_hi[:, c], wvg_lo[:, c], c == 0, c == KD - 1)
                            last.then_inc(vg_ps_done, 1)
                            pe.wait_ge(group_done, nth(ng))
                            pe.wait_ge(sc_done, nth(t - 1))
                            later = slice(i * P + CHUNK, (i + 1) * P)
                            nc.tensor.matmul(ps[:, SC, 0:P], k_in[:, g, at], q_in[:, g, at],
                                             start=True, stop=True)
                            nc.tensor.matmul(ps[:, SC, P:P + CHUNK], k_x[:, g, at], q_x[:, g, later],
                                             start=True, stop=True)
                            nc.tensor.transpose(ps[:, SC, 192:320], k_dec[:, g, at], k.ident[:])\
                                .then_inc(sc_ps_done, 1)
                            if i:
                                tile_outputs(i - 1, t - 1, g)
                            if g and i == 1:
                                transposed_outputs(ng - 1)
                        tile_outputs(GT - 1, t, g)
                    transposed_outputs(n * NG + NG - 1)
        m.end()


def project_and_route(nc, k, stage, yT_dram, w_out, x_dram, x_out, h_out, norm_w, w_group, w_expert,
                      ids_out, y_unused=None):
    W = GROUPS + E
    with ExitStack() as ctx:
        m = Memory(nc, ctx, stage)
        w_raw = m.sb("w_raw", [P, 2, 2, D])
        w_hi = m.sb("w_hi", [P, KD, D], F32R)
        w_lo = m.sb("w_lo", [P, KD, D], F32R)
        w_route = m.sb("w_route", [P, KD, W])
        src = m.sb("src", [P, 2, KD, P])
        src_hi = m.sb("src_hi", [P, 2, KD, P], F32R)
        src_lo = m.sb("src_lo", [P, 2, KD, P], F32R)
        x_old = m.sb("x_old", [P, 2, D])
        x_new = m.sb("x_new", [P, 2, D])
        h = m.sb("h", [P, 2, D])
        square = m.sb("square", [P, D])
        norm = Norm(m, k, x_new, h, square[:])
        hT = m.sb("hT", [P, KD, P])
        groups8 = m.sb("groups8", [P, 8])
        experts = m.sb("experts", [P, GROUPS, EPG])
        top_g, top_e = m.sb("top_g", [P, 8]), m.sb("top_e", [P, 8])
        at_g, at_e = m.sb("at_g", [P, 8], U32), m.sb("at_e", [P, 8], U32)
        g_no, e_no = m.sb("g_no", [P, 1]), m.sb("e_no", [P, 2])
        g_first = m.sb("g_first", [P, 1])
        minus_max = m.sb("minus_max", [P, 1])
        behind = m.sb("behind", [P, 1])
        g_exps, g_sum, e_exp = m.sb("g_exps", [P, GROUPS]), m.sb("g_sum", [P, 1]), m.sb("e_exp", [P, 1])
        denom = m.sb("denom", [P, 1])
        g_hot = m.sb("g_hot", [P, GROUPS])
        masked = m.sb("masked", [P, GROUPS, EPG])
        mine = m.sb("mine", [P, EPG])
        hot = m.sb("hot", [P, NT, 2, E])
        both = m.sb("both", [P, E], BF16)
        total = m.sb("total", [P, E])
        ranks = m.sb("ranks", [P, E])
        at_rank = m.sb("at_rank", [P, 2, E])
        rank = m.sb("rank", [P, NT, 2])
        rank_now = m.sb("rank_now", [P, 2])
        rank_int, blk_int = m.sb("rank_int", [P, 2], I32), m.sb("blk_int", [P, 2], I32)
        blk = m.sb("blk", [P, 2])
        place = m.sb("place", [P, 2])
        place_int = m.sb("place_int", [P, 2, 2], I32)
        tok = m.sb("tok", [P, 2], I32)
        zero_ids = m.sb("zero_ids", [P, E * SLOTS], I32)
        nblk, upto = m.sb("nblk", [P, E]), m.sb("upto", [P, E])
        first_row = m.sb("first_row", [P, E])
        spread, start_row = m.sb("spread", [P, NT * 2, E]), m.sb("start_row", [P, NT * 2])

        ps = m.ps("ps", [P, 8, BANK])
        HT_, LG, RK = 4, 6, 7

        w_in = [m.plain(f"w_in{j}") for j in range(2)]
        y_zeroed = m.plain("y_zeroed")
        route_in, zeroed, ids_zero = m.plain("route_in"), m.plain("zeroed"), m.plain("ids_zero")
        w_hi_done, w_lo_done = m.plain("w_hi_done"), m.sem("w_lo_done")
        src_in = [m.plain(f"src_in{j}") for j in range(2)]
        x_in = [m.plain(f"x_in{j}") for j in range(2)]
        src_hi_done, src_lo_done = m.sem("src_hi_done"), m.sem("src_lo_done")
        proj_done, x_done = m.sem("proj_done"), m.sem("x_done")
        x_stored = [m.store(f"x_stored{j}") for j in range(2)]
        h_stored = [m.store(f"h_stored{j}") for j in range(2)]
        scattered = [m.plain(f"scattered{j}") for j in range(2)]
        hT_ps_done, hT_done, logits_done = m.sem("hT_ps_done"), m.sem("hT_done"), m.sem("logits_done")
        maxima_done, exps_done = m.sem("maxima_done"), m.sem("exps_done")
        chosen_done, rank_ps_done, place_done = m.sem("chosen_done"), m.sem("rank_ps_done"), m.sem("place_done")
        order = m.plain("vector_order")
        block = m.block()

        yT = yT_dram.rearrange("(k p) t -> p k t", p=P)
        w_rows = w_out.rearrange("(a b p) c -> a p b c", b=2, p=P)

        def tiles(eng, body):
            for t in range(2):
                body(t, t)
            with eng.Fori(0, NT // 2 - 2) as q:
                for j in range(2):
                    body(q * 2 + (2 + j), j)
            for t in range(NT - 2, NT):
                body(t, t % 2)

        @block.sync
        def _(sp):
            m.prime(sp)
            sp.dma_start(norm.norm_w[:], norm_w.partition_broadcast(P)).then_inc(norm.norm_w_in, DMA)
            for a in range(4):
                if a >= 2:
                    sp.wait_ge(w_lo_done, nth(a - 2))
                sp.dma_start(w_raw[:, a % 2], w_rows[a]).then_inc(w_in[a % 2], DMA)
                if a < 2:
                    sp.dma_start(src[:, a], yT[:, :, a * P:(a + 1) * P]).then_inc(src_in[a], DMA)
                    sp.dma_start(x_old[:, a], x_dram[a * P:(a + 1) * P, :]).then_inc(x_in[a], DMA)
            with nc.allow_non_contiguous_dma(reason="16-byte rows of the group router"):
                sp.dma_start(w_route[:, :, 0:GROUPS], w_group.rearrange("(k p) c -> p k c", p=P))\
                    .then_inc(route_in, DMA)
            sp.dma_start(w_route[:, :, GROUPS:], w_expert.rearrange("(k p) c -> p k c", p=P))\
                .then_inc(route_in, DMA)

            def body(t, j):
                more = not (isinstance(t, int) and t >= NT - 2)
                if more:
                    sp.wait_ge(src_lo_done, nth(t))
                    sp.dma_start(src[:, j], yT[:, :, bass.ds(t * P + 2 * P, P)]).then_inc(src_in[j], DMA)
                sp.wait_ge(x_done, nth(t))
                sp.dma_start(x_out[bass.ds(t * P, P), :], x_new[:, j]).then_inc(x_stored[j], DMA)
                if more:
                    sp.dma_start(x_old[:, j], x_dram[bass.ds(t * P + 2 * P, P), :]).then_inc(x_in[j], DMA)
                sp.wait_ge(norm.h_done, nth(t))
                sp.dma_start(h_out[bass.ds(t * P, P), :], h[:, j]).then_inc(h_stored[j], DMA)

            tiles(sp, body)
            for j in range(2):
                sp.wait_ge(x_stored[j], nth_store(NT // 2 - 1))
                sp.wait_ge(h_stored[j], nth_store(NT // 2 - 1))

        @block.gpsimd
        def _(pool):
            pool.memset(zero_ids[:], 0).then_inc(zeroed, 1)
            pool.wait_ge(zeroed, 1)
            ids = ids_out.rearrange("(p n) o -> p (n o)", p=P)
            pool.dma_start(ids, zero_ids[:]).then_inc(ids_zero, DMA)
            pool.wait_ge(ids_zero, nth_dma(0))
            if y_unused is not None:
                pool.dma_start(y_unused.rearrange("(p n) (a c) -> p (n a) c", p=P, c=E * SLOTS),
                               zero_ids[:].bitcast(F32).unsqueeze(1)
                               .to_broadcast([P, y_unused.shape[0] // P * (D // (E * SLOTS)), E * SLOTS]))\
                    .then_inc(y_zeroed, DMA)

            def body(t, j):
                pool.wait_ge(place_done, nth(t))
                if not isinstance(t, int):
                    stand(pool)
                for c in range(2):
                    pool.indirect_dma_start(
                        ids_out, bass.IndirectOffsetOnAxis(place_int[:, j, c:c + 1].bitcast(U32), 0),
                        tok[:, j:j + 1], None).then_inc(scattered[j], DMA)

            tiles(pool, body)
            for j in range(2):
                pool.wait_ge(scattered[j], NT * DMA)
            if y_unused is not None:
                pool.wait_ge(y_zeroed, nth_dma(0))

        @block.scalar
        def _(act):
            def split(t, j, loaded):
                act.wait_ge(src_in[j], nth_dma(loaded))
                act.wait_ge(proj_done, nth(t - 2))
                nc.scalar.activation(src_hi[:, j], src[:, j], ACT.Copy).then_inc(src_hi_done, 1)

            def exps(t):
                act.wait_ge(maxima_done, nth(t))
                nc.scalar.activation(g_exps[:], groups8[:, 0:GROUPS], ACT.Exp, bias=minus_max[:],
                                     accum_out=g_sum[:])
                nc.scalar.activation(e_exp[:], behind[:], ACT.Exp).then_inc(exps_done, 1)

            for a in range(4):
                act.wait_ge(w_in[a % 2], nth_dma(a // 2))
                nc.scalar.activation(w_hi[:, 2 * a:2 * a + 2], w_raw[:, a % 2], ACT.Copy).then_inc(w_hi_done, 1)
                if a < 2:
                    split(a, a, 0)

            def body(t, j):
                act.wait_ge(x_done, nth(t))
                norm.scalar(nc, act, j, t)
                if not (isinstance(t, int) and t >= NT - 2):
                    split(t + 2, j, (t - j) // 2 + 1)
                act.wait_ge(hT_ps_done, nth(t))
                act.wait_ge(logits_done, nth(t - 1))
                for b in range(2):
                    last = nc.scalar.activation(hT[:, 4 * b:4 * b + 4],
                                                ps[:, HT_ + b].rearrange("p (a c) -> p a c", c=P), ACT.Copy)
                last.then_inc(hT_done, 1)
                if not (isinstance(t, int) and t == 0):
                    exps(t - 1)

            tiles(act, body)
            exps(NT - 1)

        @block.vector
        def _(dve):
            step = Steps(dve, order)
            step.add(nc.vector.memset(groups8[:], -3.0e38))
            step.add(nc.vector.memset(total[:], 0.0))
            step.wait()

            def split(t, j):
                dve.wait_ge(src_hi_done, nth(t))
                nc.vector.tensor_tensor(src_lo[:, j], src[:, j], src_hi[:, j].bitcast(F32), ALU.subtract)\
                    .then_inc(src_lo_done, 1)

            for a in range(4):
                dve.wait_ge(w_hi_done, a + 1)
                nc.vector.tensor_tensor(w_lo[:, 2 * a:2 * a + 2], w_raw[:, a % 2],
                                        w_hi[:, 2 * a:2 * a + 2].bitcast(F32), ALU.subtract)\
                    .then_inc(w_lo_done, 1)
                if a < 2:
                    split(a, a)
            dve.wait_ge(norm.norm_w_in, nth_dma(0))

            def choose(t):
                dve.wait_ge(logits_done, nth(t))
                step.add(nc.vector.tensor_copy(groups8[:, 0:GROUPS], ps[:, LG, 0:GROUPS]))
                nc.vector.tensor_copy(experts[:].rearrange("p g e -> p (g e)"), ps[:, LG, GROUPS:W])
                step.wait()
                stand(dve)
                step(nc.vector.max(top_g[:], groups8[:]))
                step.add(nc.vector.tensor_scalar(minus_max[:], top_g[:, 0:1], -1.0, None, ALU.mult))
                stand(dve)
                step(nc.vector.max_index(at_g[:], top_g[:], groups8[:]))
                step(nc.vector.tensor_copy(g_no[:], at_g[:, 0:1]))
                step.add(nc.vector.tensor_scalar(g_first[:], g_no[:], float(EPG), None, ALU.mult))
                step(nc.vector.tensor_scalar(g_hot[:], k.expert_no[:, 0:GROUPS], g_no[:], None, ALU.is_equal))
                step(nc.vector.tensor_tensor(masked[:], experts[:],
                                             g_hot[:].unsqueeze(2).to_broadcast([P, GROUPS, EPG]), ALU.mult))
                step(nc.vector.tensor_reduce(mine[:], masked[:].rearrange("p g e -> p e g"), AX.X, ALU.add))
                stand(dve)
                step(nc.vector.max(top_e[:], mine[:]))
                nc.vector.tensor_tensor(behind[:], top_e[:, 1:2], top_e[:, 0:1], ALU.subtract)\
                    .then_inc(maxima_done, 1)
                step(nc.vector.max_index(at_e[:], top_e[:], mine[:]))
                step(nc.vector.tensor_copy(e_no[:], at_e[:, 0:2]))
                step(nc.vector.tensor_scalar(e_no[:], e_no[:], g_first[:], None, ALU.add))
                for c in range(2):
                    step.add(nc.vector.tensor_scalar(hot[:, bass.ds(t, 1), c], k.expert_no[:].unsqueeze(1),
                                                     e_no[:, c:c + 1], None, ALU.is_equal))
                step.wait()
                nc.vector.tensor_tensor(both[:].unsqueeze(1), hot[:, bass.ds(t, 1), 0],
                                        hot[:, bass.ds(t, 1), 1], ALU.add).then_inc(chosen_done, 1)

            CHOOSE = 15

            def place_tokens(t, j):
                dve.wait_ge(exps_done, nth(t))
                step(nc.vector.tensor_scalar(denom[:], e_exp[:], 1.0, g_sum[:], ALU.add, ALU.mult))
                step(nc.vector.reciprocal(denom[:], denom[:]))
                nc.vector.tensor_copy(k.weight[:, bass.ds(t, 1), 0], denom[:])
                nc.vector.tensor_tensor(k.weight[:, bass.ds(t, 1), 1], denom[:], e_exp[:], ALU.mult)
                dve.wait_ge(rank_ps_done, nth(t))
                step(nc.vector.tensor_tensor(ranks[:], ps[:, RK, 0:E], total[:], ALU.add))
                step.add(nc.vector.tensor_tensor(total[:], ps[:, RK, E:2 * E], total[:], ALU.add))
                step(nc.vector.tensor_tensor(at_rank[:].unsqueeze(1), hot[:, bass.ds(t, 1)],
                                             ranks[:].unsqueeze(1).unsqueeze(1).to_broadcast([P, 1, 2, E]),
                                             ALU.mult))
                step(nc.vector.tensor_reduce(rank_now[:], at_rank[:], AX.X, ALU.add))
                step.add(nc.vector.tensor_copy(rank[:, bass.ds(t, 1)], rank_now[:].unsqueeze(1)))
                step(nc.vector.tensor_copy(rank_int[:], rank_now[:]))
                step(nc.vector.tensor_scalar(blk_int[:], rank_int[:], 7, None, ALU.logical_shift_right))
                step(nc.vector.tensor_copy(blk[:], blk_int[:]))
                step(nc.vector.tensor_scalar(place[:], rank_now[:], float(E * SLOTS), None, ALU.mult))
                step(nc.vector.scalar_tensor_tensor(out=place[:], in0=blk[:], scalar=1.0 - P * E * SLOTS,
                                                    in1=place[:], op0=ALU.mult, op1=ALU.add))
                step(nc.vector.tensor_tensor(at_rank[:].unsqueeze(1), hot[:, bass.ds(t, 1)],
                                             k.expert_no[:].unsqueeze(1).unsqueeze(1)
                                             .to_broadcast([P, 1, 2, E]), ALU.mult))
                step(nc.vector.tensor_reduce(rank_now[:], at_rank[:], AX.X, ALU.add))
                step(nc.vector.scalar_tensor_tensor(out=place[:], in0=rank_now[:], scalar=float(SLOTS),
                                                    in1=place[:], op0=ALU.mult, op1=ALU.add))
                if not (isinstance(t, int) and t < 2):
                    dve.wait_ge(scattered[j], (t - j) * DMA)
                nc.vector.tensor_copy(tok[:, j:j + 1], k.token[:, bass.ds(t, 1)])
                nc.vector.tensor_copy(place_int[:, j], place[:]).then_inc(place_done, 1)

            PLACE = 15
            first = step.n

            def counted(t):
                if isinstance(t, int) and t < 2:
                    return first + 0 if t == 0 else first + 1
                return t * (1 + CHOOSE + PLACE) + (first + 2 + CHOOSE - 2 * (1 + CHOOSE + PLACE))

            def body(t, j):
                step.loop(counted(t))
                dve.wait_ge(proj_done, nth(t))
                dve.wait_ge(x_in[j], nth_dma((t - j) // 2))
                dve.wait_ge(x_stored[j], nth_store((t - j) // 2 - 1))
                dve.wait_ge(norm.h_done, nth(t - 2))
                nc.vector.tensor_tensor(x_new[:, j].rearrange("p (b c) -> p b c", b=2),
                                        ps[:, 2 * j:2 * j + 2],
                                        x_old[:, j].rearrange("p (b c) -> p b c", b=2), ALU.add)\
                    .then_inc(x_done, 1)
                dve.wait_ge(x_done, nth(t))
                dve.wait_ge(h_stored[j], nth_store((t - j) // 2 - 1))
                dve.wait_ge(hT_ps_done, nth(t - 2))
                norm.vector(nc, dve, step, j, t)
                static = isinstance(t, int)
                if not (static and t >= NT - 2):
                    split(t + 2, j)
                if not (static and t < 2):
                    place_tokens(t - 2, j)
                if not (static and t < 1):
                    choose(t - 1)

            tiles(dve, body)
            place_tokens(NT - 2, 0)
            choose(NT - 1)
            place_tokens(NT - 1, 1)
            step(nc.vector.tensor_scalar(nblk[:], total[:], float(P - 1), None, ALU.add))
            step(nc.vector.tensor_copy(k.blocks[:], nblk[:]))
            step(nc.vector.tensor_scalar(k.block_at[:], k.blocks[:], 7, None, ALU.logical_shift_right))
            step(nc.vector.tensor_copy(nblk[:], k.block_at[:]))
            step(nc.vector.tensor_scalar(nblk[:], nblk[:], 1.0, None, ALU.max))
            step(nc.vector.tensor_tensor_scan(upto[:], k.ones_row[:], nblk[:], 0.0, ALU.mult, ALU.add))
            step(nc.vector.tensor_tensor(upto[:], upto[:], nblk[:], ALU.subtract))
            step.add(nc.vector.tensor_copy(k.blocks[:], nblk[:]))
            step.add(nc.vector.tensor_copy(k.block_at[:], upto[:]))
            step(nc.vector.tensor_scalar(first_row[:], upto[:], 1.0, float(P), ALU.add, ALU.mult))
            step(nc.vector.tensor_tensor(spread[:], hot[:].rearrange("p t c e -> p (t c) e"),
                                         first_row[:].unsqueeze(1).to_broadcast([P, NT * 2, E]), ALU.mult))
            step(nc.vector.tensor_reduce(start_row[:], spread[:], AX.X, ALU.add))
            step(nc.vector.tensor_tensor(rank[:].rearrange("p t c -> p (t c)"), start_row[:],
                                         rank[:].rearrange("p t c -> p (t c)"), ALU.add))
            step(nc.vector.tensor_copy(k.row[:], rank[:]))

        @block.tensor
        def _(pe):
            def project(t, j, half):
                if half == 0:
                    pe.wait_ge(src_lo_done, nth(t))
                    pe.wait_ge(x_done, nth(t - 2))
                for c in range(KD):
                    last = matmul3(nc, ps[:, 2 * j + half], src_hi[:, j, c], src_lo[:, j, c],
                                   w_hi[:, c, half * BANK:(half + 1) * BANK],
                                   w_lo[:, c, half * BANK:(half + 1) * BANK], c == 0, c == KD - 1)
                return last

            def rank_within(t):
                pe.wait_ge(chosen_done, nth(t))
                pe.wait_ge(place_done, nth(t - 1))
                nc.tensor.matmul(ps[:, RK, 0:E], k.before[:], both[:], start=True, stop=True)
                nc.tensor.matmul(ps[:, RK, E:2 * E], k.ones_bf[:], both[:], start=True, stop=True)\
                    .then_inc(rank_ps_done, 1)

            pe.wait_ge(w_lo_done, nth(3))
            pe.wait_ge(route_in, nth_dma(1))
            project(0, 0, 0)
            project(0, 0, 1).then_inc(proj_done, 1)

            def body(t, j):
                static = isinstance(t, int)
                if not (static and t == NT - 1):
                    project(t + 1, 1 - j, 0)
                pe.wait_ge(norm.h_done, nth(t))
                pe.wait_ge(hT_done, nth(t - 1))
                for c in range(KD):
                    last = nc.tensor.transpose(ps[:, HT_ + c // 4, (c % 4) * P:(c % 4 + 1) * P],
                                               h[:, j, c * P:(c + 1) * P], k.ident[:])
                last.then_inc(hT_ps_done, 1)
                if not (static and t == NT - 1):
                    project(t + 1, 1 - j, 1).then_inc(proj_done, 1)
                pe.wait_ge(hT_done, nth(t))
                pe.wait_ge(chosen_done, nth(t - 1))
                for c in range(KD):
                    last = nc.tensor.matmul(ps[:, LG, 0:W], hT[:, c], w_route[:, c], start=c == 0,
                                            stop=c == KD - 1)
                last.then_inc(logits_done, 1)
                if not (static and t == 0):
                    rank_within(t - 1)

            tiles(pe, body)
            rank_within(NT - 1)
        m.end()


def experts(nc, k, stage, h_rows, ids_dram, w_gate, w_up, w_down, y_rows):
    with ExitStack() as ctx:
        m = Memory(nc, ctx, stage)
        gu_raw = m.sb("gu_raw", [P, 2, KD, 2 * FF])
        wd_raw = m.sb("wd_raw", [P, 2, KF, D])
        gu_hi = m.sb("gu_hi", [P, 2, KD, 2 * FF], F32R)
        gu_lo = m.sb("gu_lo", [P, 2, KD, 2 * FF], F32R)
        wd_hi = m.sb("wd_hi", [P, 2, KF, D], F32R)
        wd_lo = m.sb("wd_lo", [P, 2, KF, D], F32R)
        ids = m.sb("ids", [P, E * SLOTS], I32)
        ids_now = m.sb("ids_now", [P, 1], I32)
        rows = m.sb("rows", [P, D])
        hT_hi = m.sb("hT_hi", [P, KD, P], F32R)
        hT_lo = m.sb("hT_lo", [P, KD, P], F32R)
        silu = m.sb("silu", [P, FF])
        act_ = m.sb("act", [P, FF])
        aT_hi = m.sb("aT_hi", [P, KF, P], F32R)
        aT_lo = m.sb("aT_lo", [P, KF, P], F32R)
        y = m.sb("y", [P, D])

        ps = m.ps("ps", [P, 8, BANK])
        GU, HT_, AT, Y = 0, 1, 3, 4

        gate_in, up_in, wd_in, ids_in = (m.plain(s) for s in ("gate_in", "up_in", "wd_in", "ids_in"))
        zeroed = m.plain("zeroed")
        gu_hi_done, gu_lo_done = m.sem("gu_hi_done"), m.sem("gu_lo_done")
        wd_hi_done, wd_lo_done = m.sem("wd_hi_done"), m.sem("wd_lo_done")
        ids_set, rows_in = m.sem("ids_set"), m.plain("rows_in")
        hT_ps_done, hT_hi_done, hT_lo_done = m.sem("hT_ps_done"), m.sem("hT_hi_done"), m.sem("hT_lo_done")
        gu_ps_done, silu_done, act_done = m.sem("gu_ps_done"), m.sem("silu_done"), m.sem("act_done")
        aT_ps_done, aT_hi_done, aT_lo_done = m.sem("aT_ps_done"), m.sem("aT_hi_done"), m.sem("aT_lo_done")
        y_ps_done, y_done, y_stored = m.sem("y_ps_done"), m.sem("y_done"), m.store("y_stored")
        block = m.block()

        def expert_blocks(eng, each, before=None, behind=None):
            def one(e, at):
                s = eng.value_load(k.block_at[0:1, at], min_val=0, max_val=MAX_BLOCKS - 1)
                n = eng.value_load(k.blocks[0:1, at], min_val=1, max_val=SLOTS)
                with eng.Fori(0, n) as b:
                    each(e, b, nc.s_assert_within(s + b, min_val=0, max_val=MAX_BLOCKS - 1))
                return s, n

            with eng.Fori(0, E - 1) as e:
                if before:
                    before(e)
                one(e, bass.ds(e, 1))
                if behind:
                    behind(e)
            s, n = one(E - 1, slice(E - 1, E))
            return nc.s_assert_within(s + n, min_val=1, max_val=MAX_BLOCKS)

        def slot(e):
            return bass.ds(e % 2, 1)

        @block.sync
        def _(sp):
            m.prime(sp)
            sp.dma_start(ids[:], ids_dram.rearrange("(p n) o -> p (n o)", p=P)).then_inc(ids_in, DMA)

            def load(e):
                parts = ((gate_in, gu_raw[:, slot(e), :, 0:FF], w_gate), (up_in, gu_raw[:, slot(e), :, FF:], w_up),
                         (wd_in, wd_raw[:, slot(e)], w_down))
                for landed, into, w in parts:
                    if not (isinstance(e, int) and e == 0):
                        sp.wait_ge(landed, nth_dma(e - 1))
                    sp.dma_start(into, w[bass.ds(e, 1)].rearrange("e (k p) c -> p e k c", p=P))\
                        .then_inc(landed, DMA)

            load(0)
            load(1)
            with sp.Fori(0, E - 2) as e:
                sp.wait_ge(gu_lo_done, nth(e))
                sp.wait_ge(wd_lo_done, nth(e))
                load(e + 2)

        @block.gpsimd
        def _(pool):
            pool.memset(aT_hi[:].bitcast(F32), 0.0)
            pool.memset(aT_lo[:].bitcast(F32), 0.0)
            pool.memset(wd_hi[:, 1].bitcast(F32), 0.0)
            pool.memset(wd_lo[:, 1].bitcast(F32), 0.0).then_inc(zeroed, 1)
            pool.wait_ge(ids_in, nth_dma(0))

            def gather(column, g):
                pool.wait_ge(hT_ps_done, nth(g - 1))
                stand(pool)
                pool.tensor_copy(ids_now[:], ids[:, bass.ds(column, 1)]).then_inc(ids_set, 1)
                pool.wait_ge(ids_set, nth(g))
                stand(pool)
                pool.indirect_dma_start(rows[:], None, h_rows,
                                        bass.IndirectOffsetOnAxis(ids_now[:].bitcast(U32), 0))\
                    .then_inc(rows_in, DMA)

            blocks = expert_blocks(pool, lambda e, b, g: gather(e * SLOTS + b, g))
            gather(0, blocks)
            pool.wait_ge(rows_in, nth_dma(blocks))

        @block.scalar
        def _(act):
            def split_gu(e):
                act.wait_ge(gate_in, nth_dma(e))
                act.wait_ge(up_in, nth_dma(e))
                stand(act)
                nc.scalar.activation(gu_hi[:, slot(e)], gu_raw[:, slot(e)], ACT.Copy).then_inc(gu_hi_done, 1)

            def split_wd(e):
                act.wait_ge(wd_in, nth_dma(e))
                stand(act)
                nc.scalar.activation(wd_hi[:, slot(e)], wd_raw[:, slot(e)], ACT.Copy).then_inc(wd_hi_done, 1)

            def take_rows(g):
                act.wait_ge(hT_ps_done, nth(g))
                for b in range(2):
                    nc.scalar.activation(hT_hi[:, 4 * b:4 * b + 4],
                                         ps[:, HT_ + b].rearrange("p (a c) -> p a c", c=P), ACT.Copy)\
                        .then_inc(hT_hi_done, 1)

            def take_y(g):
                act.wait_ge(y_ps_done, nth(g))
                act.wait_ge(y_stored, nth_store(g - 1))
                nc.scalar.activation(y[:].rearrange("p (b c) -> p b c", b=2), ps[:, Y:Y + 2], ACT.Copy)\
                    .then_inc(y_done, 1)

            def store_y(g):
                act.wait_ge(y_done, nth(g))
                act.dma_start(y_rows[bass.ds(g * P, P), :], y[:]).then_inc(y_stored, DMA)

            act.wait_ge(zeroed, 1)
            split_gu(0)
            split_wd(0)
            take_rows(0)

            def each(e, b, g):
                act.wait_ge(gu_ps_done, nth(g))
                act.wait_ge(act_done, nth(g - 1))
                nc.scalar.activation(silu[:], ps[:, GU, 0:FF], ACT.Silu).then_inc(silu_done, 1)
                take_rows(g + 1)
                take_y(g)
                act.wait_ge(aT_ps_done, nth(g))
                nc.scalar.activation(aT_hi[:], ps[:, AT, 0:FF].rearrange("p (a c) -> p a c", c=P), ACT.Copy)\
                    .then_inc(aT_hi_done, 1)
                store_y(g)

            blocks = expert_blocks(act, each, lambda e: split_gu(e + 1), lambda e: split_wd(e + 1))
            take_y(blocks)
            store_y(blocks)
            act.wait_ge(y_stored, nth_store(blocks))
            stand(act)

        @block.vector
        def _(dve):
            def split_gu(e):
                dve.wait_ge(gu_hi_done, nth(e))
                nc.vector.tensor_tensor(gu_lo[:, slot(e)], gu_raw[:, slot(e)],
                                        gu_hi[:, slot(e)].bitcast(F32), ALU.subtract).then_inc(gu_lo_done, 1)

            def split_wd(e):
                dve.wait_ge(wd_hi_done, nth(e))
                nc.vector.tensor_tensor(wd_lo[:, slot(e)], wd_raw[:, slot(e)],
                                        wd_hi[:, slot(e)].bitcast(F32), ALU.subtract).then_inc(wd_lo_done, 1)

            def take_rows(g):
                for b in range(2):
                    dve.wait_ge(hT_hi_done, nth(2 * g + b))
                    last = nc.vector.tensor_tensor(
                        hT_lo[:, 4 * b:4 * b + 4], ps[:, HT_ + b].rearrange("p (a c) -> p a c", c=P),
                        hT_hi[:, 4 * b:4 * b + 4].bitcast(F32), ALU.subtract)
                last.then_inc(hT_lo_done, 1)

            split_gu(0)
            split_wd(0)
            take_rows(0)

            def each(e, b, g):
                dve.wait_ge(silu_done, nth(g))
                nc.vector.tensor_tensor(act_[:], silu[:], ps[:, GU, FF:], ALU.mult).then_inc(act_done, 1)
                take_rows(g + 1)
                dve.wait_ge(aT_hi_done, nth(g))
                nc.vector.tensor_tensor(aT_lo[:], ps[:, AT, 0:FF].rearrange("p (a c) -> p a c", c=P),
                                        aT_hi[:].bitcast(F32), ALU.subtract).then_inc(aT_lo_done, 1)

            expert_blocks(dve, each, lambda e: split_gu(e + 1), lambda e: split_wd(e + 1))

        @block.tensor
        def _(pe):
            def transpose_rows(g):
                pe.wait_ge(rows_in, nth_dma(g))
                pe.wait_ge(hT_lo_done, nth(g - 1))
                for c in range(KD):
                    last = nc.tensor.transpose(ps[:, HT_ + c // 4, (c % 4) * P:(c % 4 + 1) * P],
                                               rows[:, c * P:(c + 1) * P], k.ident[:])
                last.then_inc(hT_ps_done, 1)

            def down(g, e):
                pe.wait_ge(aT_lo_done, nth(g - 1))
                pe.wait_ge(wd_lo_done, nth(e))
                pe.wait_ge(y_done, nth(g - 1))
                for half in range(2):
                    cols = slice(half * BANK, (half + 1) * BANK)
                    for c in range(KF):
                        last = matmul3(nc, ps[:, Y + half], aT_hi[:, c], aT_lo[:, c],
                                       wd_hi[:, bass.ds((e + 2) % 2, 1), c, cols],
                                       wd_lo[:, bass.ds((e + 2) % 2, 1), c, cols], c == 0, c == KF - 1)
                last.then_inc(y_ps_done, 1)

            pe.wait_ge(zeroed, 1)
            transpose_rows(0)

            def each(e, b, g):
                pe.wait_ge(gu_lo_done, nth(e))
                pe.wait_ge(hT_lo_done, nth(g))
                pe.wait_ge(act_done, nth(g - 1))
                for c in range(KD):
                    last = matmul3(nc, ps[:, GU], hT_hi[:, c], hT_lo[:, c], gu_hi[:, slot(e), c],
                                   gu_lo[:, slot(e), c], c == 0, c == KD - 1)
                last.then_inc(gu_ps_done, 1)
                transpose_rows(g + 1)
                down(g, e + ((b + (SLOTS - 1)) // SLOTS) - 1)
                pe.wait_ge(act_done, nth(g))
                pe.wait_ge(aT_lo_done, nth(g - 1))
                for c in range(KF):
                    last = nc.tensor.transpose(ps[:, AT, c * P:(c + 1) * P], act_[:, c * P:(c + 1) * P],
                                               k.ident[:])
                last.then_inc(aT_ps_done, 1)

            blocks = expert_blocks(pe, each)
            down(blocks, E - 1)
        m.end()


class Combine:

    def __init__(self, m, k, x, h, square, y_a, y_b):
        self.k, self.y = k, (y_a, y_b)
        self.norm = Norm(m, k, x, h, square)
        self.row_now = m.sb("row_now", [P, 2, 2], I32)
        self.weight_now = m.sb("weight_now", [P, 2])
        self.row_set = m.sem("row_set")
        self.x_in = [m.plain(f"x_in{j}") for j in range(2)]
        self.y_in = [m.plain(f"y_in{j}") for j in range(2)]
        self.x_done = m.sem("x_done")

    def pool(self, nc, pool, y_rows, j, t, q):
        pool.wait_ge(self.x_done, nth(t - 2))
        stand(pool)
        pool.tensor_copy(self.row_now[:, j:j + 1], self.k.row[:, bass.ds(t, 1)]).then_inc(self.row_set, 1)
        pool.wait_ge(self.row_set, nth(t))
        stand(pool)
        for c in range(2):
            pool.indirect_dma_start(self.y[c][:, j], None, y_rows,
                                    bass.IndirectOffsetOnAxis(self.row_now[:, j, c:c + 1].bitcast(U32), 0))\
                .then_inc(self.y_in[j], DMA)

    def scalar(self, nc, act, j, t):
        act.wait_ge(self.x_done, nth(t))
        self.norm.scalar(nc, act, j, t)

    STEPS = 3

    def vector(self, nc, dve, step, j, t, q):
        x = self.norm.x
        stand(dve)
        step(nc.vector.tensor_copy(self.weight_now[:].unsqueeze(1), self.k.weight[:, bass.ds(t, 1)]))
        dve.wait_ge(self.x_in[j], nth_dma(q))
        dve.wait_ge(self.y_in[j], nth_dma(2 * q + 1))
        step(nc.vector.scalar_tensor_tensor(out=x[:, j], in0=self.y[0][:, j], scalar=self.weight_now[:, 0:1],
                                            in1=x[:, j], op0=ALU.mult, op1=ALU.add))
        nc.vector.scalar_tensor_tensor(out=x[:, j], in0=self.y[1][:, j], scalar=self.weight_now[:, 1:2],
                                       in1=x[:, j], op0=ALU.mult, op1=ALU.add).then_inc(self.x_done, 1)
        dve.wait_ge(self.x_done, nth(t))
        self.norm.vector(nc, dve, step, j, t)


def lru(nc, k, x_dram, y_rows, x_out, norm_w, w_in, conv_w, conv_b, w_r, b_r, w_i, b_i, lam, yT_dram):
    with ExitStack() as ctx:
        m = Memory(nc, ctx, "lru")
        hT_hi = m.sb("hT_hi", [P, KD, TH], F32R)
        hT_lo = m.sb("hT_lo", [P, KD, TH], F32R)
        work = m.sb("work", [P, 4, D])
        shared = m.sb("shared", [P, 4, D])
        square = m.sb("square", [P, D])
        cb = Combine(m, k, work[:, 0:2], work[:, 2:4], square[:], shared[:, 0:2], shared[:, 2:4])
        norm = cb.norm

        def part(at):
            return shared[:, at].rearrange("p (c t) -> p c t", c=LCT)

        r, inp, s_, a = part(0), part(1), part(2), part(3)
        kinds = []
        for name, shape in (("wx", [P, KD, LBW]), ("wg", [P, KD, LBW]), ("wr", [P, 2, LCT, LBW])):
            kinds.append(dict(raw=m.sb(name + "_raw", shape), hi=m.sb(name + "_hi", shape, F32R),
                              lo=m.sb(name + "_lo", shape, F32R), landed=m.plain(name + "_in"),
                              hi_done=m.sem(name + "_hi_done"), lo_done=m.sem(name + "_lo_done")))
        wx, wg, wr = kinds
        CB, BR, BI, SP, MSP = TAPS, TAPS + 1, TAPS + 2, TAPS + 3, TAPS + 4
        par = m.sb("par", [P, LRU_BLOCKS * LCT, MSP + 1])
        mine = m.sb("mine", [P, LCT, MSP + 1])
        soft = m.sb("soft", [P, LRU_BLOCKS * LCT])
        xb = m.sb("xb", [P, LCT, TAPS - 1 + GROUP])
        xc = m.sb("xc", [P, LCT, GROUP])
        xc_hi = m.sb("xc_hi", [P, LCT, GROUP], F32R)
        xc_lo = m.sb("xc_lo", [P, LCT, GROUP], F32R)
        gate = m.sb("gate", [P, LCT, GROUP])
        hs = m.sb("hs", [P, LCT, GROUP])
        y = m.sb("y", [P, LCT, GROUP])
        tail = m.sb("tail", [P, LRU_BLOCKS * LCT, TAPS - 1])
        last_h = m.sb("last_h", [P, LRU_BLOCKS * LCT])
        h_start = m.sb("h_start", [P, LCT])

        ps = m.ps("ps", [P, 8, BANK])
        XB, GB, RG, IG = 0, 2, 4, 6

        par_in = m.plain("par_in")
        par_done, soft_done = m.plain("par_done"), m.plain("soft_done")
        x_stored = [m.store(f"x_stored{j}") for j in range(2)]
        hT_ps_done, hT_hi_done, hT_lo_done = m.sem("hT_ps_done"), m.sem("hT_hi_done"), m.sem("hT_lo_done")
        xb_ps_done, xb_done, conv_done = m.sem("xb_ps_done"), m.sem("xb_done"), m.sem("conv_done")
        xc_hi_done, xc_lo_done = m.sem("xc_hi_done"), m.sem("xc_lo_done")
        gb_ps_done, gate_done = m.sem("gb_ps_done"), m.sem("gate_done")
        rg_ps_done, rg_done, decay_done = m.sem("rg_ps_done"), m.sem("rg_done"), m.sem("decay_done")
        ratio_done, mult_done, y_done = m.sem("ratio_done"), m.sem("mult_done"), m.sem("y_done")
        y_stored = m.store("y_stored")
        order = m.plain("vector_order")
        block = m.block()

        w_rows = w_in.rearrange("(k p) c -> p k c", p=P)
        NBLK = HALVES * LRU_BLOCKS

        @block.sync
        def _(sp):
            m.prime(sp)

            def load(kind, nb):
                if kind is wr:
                    for c, w in enumerate((w_r, w_i)):
                        sp.dma_start(wr["raw"][:, c:c + 1], w[bass.ds(nb, 1)]
                                     .rearrange("n (k p) c -> p n k c", p=P)).then_inc(wr["landed"], DMA)
                else:
                    first = 0 if kind is wx else D
                    sp.dma_start(kind["raw"][:], w_rows[:, :, bass.ds(nb * LBW + first, LBW)])\
                        .then_inc(kind["landed"], DMA)

            sp.dma_start(norm.norm_w[:], norm_w.partition_broadcast(P)).then_inc(norm.norm_w_in, DMA)
            for i in range(2):
                sp.dma_start(norm.x[:, i], x_dram[i * P:(i + 1) * P, :]).then_inc(cb.x_in[i], DMA)
            with nc.allow_non_contiguous_dma(reason="a few parameters of each channel"):
                for tap in range(TAPS):
                    sp.dma_start(par[:, :, tap], conv_w[tap].rearrange("(c p) -> p c", p=P)).then_inc(par_in, DMA)
                for at, v in ((CB, conv_b), (BR, b_r), (BI, b_i), (SP, lam)):
                    sp.dma_start(par[:, :, at], v.rearrange("(c p) -> p c", p=P)).then_inc(par_in, DMA)
            for kind in kinds:
                load(kind, 0)
            with sp.Fori(0, HALVES) as half:
                for i in range(HT):
                    t = half * HT + i
                    sp.wait_ge(cb.x_done, nth(t))
                    sp.dma_start(x_out[bass.ds(t * P, P), :], norm.x[:, i % 2]).then_inc(x_stored[i % 2], DMA)
                    if i < HT - 2:
                        sp.wait_ge(norm.h_done, nth(t))
                        sp.wait_ge(x_stored[i % 2], nth_store(half * (HT // 2) + i // 2))
                        sp.dma_start(norm.x[:, i % 2], x_dram[bass.ds(t * P + 2 * P, P), :])\
                            .then_inc(cb.x_in[i % 2], DMA)
                for i in range(2):
                    sp.wait_ge(norm.h_done, nth(half * HT + (HT - 2 + i)))
                    sp.wait_ge(x_stored[i], nth_store(half * (HT // 2) + (HT // 2 - 1)))
                    sp.dma_start(norm.x[:, i], x_dram[bass.ds(((half + 1) % HALVES) * TH + i * P, P), :])\
                        .then_inc(cb.x_in[i], DMA)
                with sp.Fori(0, LRU_BLOCKS) as b:
                    n = half * LRU_BLOCKS + b
                    for kind in kinds:
                        sp.wait_ge(kind["lo_done"], nth(n))
                        load(kind, (b + 1) % LRU_BLOCKS)
                    for g in range(NG):
                        sp.wait_ge(y_done, nth(n * NG + g))
                        sp.dma_start(yT_dram[bass.ds(b * LBW, LBW), bass.ds(half * TH + g * GROUP, GROUP)]
                                     .rearrange("(c p) t -> p c t", p=P), y[:]).then_inc(y_stored, DMA)
            sp.wait_ge(y_stored, nth_store(NBLK * NG - 1))
            sp.wait_ge(wx["landed"], nth_dma(NBLK))
            sp.wait_ge(wg["landed"], nth_dma(NBLK))
            sp.wait_ge(wr["landed"], nth_dma(2 * NBLK + 1))
            for i in range(2):
                sp.wait_ge(cb.x_in[i], nth_dma(NT // 2))

        @block.gpsimd
        def _(pool):
            with pool.Fori(0, HALVES) as half:
                pool.wait_ge(y_done, nth(half * (LRU_BLOCKS * NG) - 1))
                stand(pool)
                for i in range(HT):
                    cb.pool(nc, pool, y_rows, i % 2, half * HT + i, None)

        @block.scalar
        def _(act):
            def split(kind, n):
                act.wait_ge(kind["landed"], nth_dma(2 * n + 1 if kind is wr else n))
                nc.scalar.activation(kind["hi"][:], kind["raw"][:], ACT.Copy).then_inc(kind["hi_done"], 1)

            act.wait_ge(par_in, nth_dma(TAPS + 3))
            nc.scalar.activation(soft[:], par[:, :, SP], ACT.Abs).then_inc(soft_done, 1)
            act.wait_ge(soft_done, 1)
            nc.scalar.activation(soft[:], soft[:], ACT.Exp, scale=-1.0).then_inc(soft_done, 1)
            act.wait_ge(soft_done, 2)
            nc.scalar.activation(soft[:], soft[:], ACT.Ln, bias=1.0).then_inc(soft_done, 1)
            for kind in kinds:
                split(kind, 0)
            with act.Fori(0, HALVES) as half:
                for i in range(HT):
                    t = half * HT + i
                    cb.scalar(nc, act, i % 2, t)
                    act.wait_ge(hT_ps_done, nth(t))
                    for b in range(2):
                        nc.scalar.activation(hT_hi[:, 4 * b:4 * b + 4, i * P:(i + 1) * P],
                                             ps[:, 2 * (i % 2) + b].rearrange("p (a c) -> p a c", c=P),
                                             ACT.Copy).then_inc(hT_hi_done, 1)
                with act.Fori(0, LRU_BLOCKS) as b:
                    n = half * LRU_BLOCKS + b
                    for g in range(NG):
                        q = n * NG + g
                        act.wait_ge(xb_ps_done, nth(q))
                        act.wait_ge(conv_done, nth(q - 1))
                        nc.scalar.activation(xb[:, :, TAPS - 1:], ps[:, XB:XB + 2], ACT.Copy)\
                            .then_inc(xb_done, 1)
                        act.wait_ge(conv_done, nth(q))
                        nc.scalar.activation(xc_hi[:], xc[:], ACT.Copy).then_inc(xc_hi_done, 1)
                        if g == NG - 1:
                            split(wx, n + 1)
                        act.wait_ge(gb_ps_done, nth(q))
                        act.wait_ge(y_done, nth(q - 1))
                        nc.scalar.activation(gate[:], ps[:, GB:GB + 2], ACT.Gelu_apprx_tanh)\
                            .then_inc(gate_done, 1)
                        if g == NG - 1:
                            split(wg, n + 1)
                        act.wait_ge(rg_ps_done, nth(q))
                        act.wait_ge(decay_done, nth(q - 1))
                        for c in range(LCT):
                            nc.scalar.activation(r[:, c], ps[:, RG + c], ACT.Sigmoid, bias=mine[:, c, BR:BR + 1])
                            last = nc.scalar.activation(inp[:, c], ps[:, IG + c], ACT.Sigmoid,
                                                        bias=mine[:, c, BI:BI + 1])
                        last.then_inc(rg_done, 1)
                        if g == NG - 1:
                            split(wr, n + 1)
                        act.wait_ge(rg_done, nth(q))
                        for c in range(LCT):
                            nc.scalar.activation(s_[:, c], r[:, c], ACT.Tanh, scale=mine[:, c, SP:SP + 1])
                        for c in range(LCT):
                            last = nc.scalar.activation(a[:, c], r[:, c], ACT.Exp, scale=mine[:, c, MSP:MSP + 1])
                        last.then_inc(decay_done, 1)
                        act.wait_ge(ratio_done, nth(q))
                        nc.scalar.activation(s_, s_, ACT.Sqrt, scale=2.0).then_inc(mult_done, 1)

        @block.vector
        def _(dve):
            step = Steps(dve, order)
            step.add(nc.vector.memset(tail[:], 0.0))
            step.add(nc.vector.memset(last_h[:], 0.0))
            step.wait()
            dve.wait_ge(par_in, nth_dma(TAPS + 3))
            dve.wait_ge(soft_done, 3)
            step(nc.vector.tensor_scalar(par[:, :, SP], par[:, :, SP], -1.0, 0.0, ALU.mult, ALU.max))
            step(nc.vector.tensor_tensor(par[:, :, SP], par[:, :, SP], soft[:], ALU.add))
            step(nc.vector.tensor_scalar(par[:, :, MSP], par[:, :, SP], -LRU_C, None, ALU.mult))
            step(nc.vector.tensor_scalar(par[:, :, SP], par[:, :, SP], LRU_C, None, ALU.mult))
            dve.wait_ge(norm.norm_w_in, nth_dma(0))

            def split(kind, n):
                dve.wait_ge(kind["hi_done"], nth(n))
                nc.vector.tensor_tensor(kind["lo"][:], kind["raw"][:], kind["hi"][:].bitcast(F32), ALU.subtract)\
                    .then_inc(kind["lo_done"], 1)

            for kind in kinds:
                split(kind, 0)
            first = step.n
            IN_NORM = HT * Combine.STEPS
            IN_BLOCK = LRU_STEPS
            with dve.Fori(0, HALVES) as half:
                step.loop(half * (IN_NORM + LRU_BLOCKS * IN_BLOCK) + first)
                for i in range(HT):
                    t = half * HT + i
                    dve.wait_ge(hT_ps_done, nth(t - 2))
                    cb.vector(nc, dve, step, i % 2, t, half * (HT // 2) + i // 2)
                    for b in range(2):
                        dve.wait_ge(hT_hi_done, nth(2 * t + b))
                        part_ = (slice(None), slice(4 * b, 4 * b + 4), slice(i * P, (i + 1) * P))
                        last = nc.vector.tensor_tensor(
                            hT_lo[part_], ps[:, 2 * (i % 2) + b].rearrange("p (a c) -> p a c", c=P),
                            hT_hi[part_].bitcast(F32), ALU.subtract)
                    last.then_inc(hT_lo_done, 1)
                with dve.Fori(0, LRU_BLOCKS) as b:
                    n = half * LRU_BLOCKS + b
                    step.loop(half * (IN_NORM + LRU_BLOCKS * IN_BLOCK) + b * IN_BLOCK + (first + IN_NORM))
                    channels = bass.ds(b * LCT, LCT)
                    stand(dve)
                    step(nc.vector.tensor_copy(mine[:], par[:, channels]))
                    for g in range(NG):
                        q = n * NG + g
                        stand(dve)
                        step.add(nc.vector.tensor_copy(xb[:, :, 0:TAPS - 1], tail[:, channels]))
                        dve.wait_ge(xb_done, nth(q))
                        step.wait()
                        for c in range(LCT):
                            step.add(nc.vector.tensor_scalar(
                                xc[:, c], xb[:, c, 0:GROUP], mine[:, c, 0:1], mine[:, c, CB:CB + 1],
                                ALU.mult, ALU.add))
                        step.add(nc.vector.tensor_copy(tail[:, channels], xb[:, :, GROUP:]))
                        step.wait()
                        for tap in range(1, TAPS):
                            for c in range(LCT):
                                last = nc.vector.scalar_tensor_tensor(
                                    out=xc[:, c], in0=xb[:, c, tap:tap + GROUP], scalar=mine[:, c, tap:tap + 1],
                                    in1=xc[:, c], op0=ALU.mult, op1=ALU.add)
                                if tap < TAPS - 1:
                                    step.add(last)
                            if tap < TAPS - 1:
                                step.wait()
                        last.then_inc(conv_done, 1)
                        dve.wait_ge(xc_hi_done, nth(q))
                        nc.vector.tensor_tensor(xc_lo[:], xc[:], xc_hi[:].bitcast(F32), ALU.subtract)\
                            .then_inc(xc_lo_done, 1)
                        if g == NG - 1:
                            for kind in kinds:
                                split(kind, n + 1)
                        step.add(nc.vector.tensor_copy(h_start[:].unsqueeze(2), last_h[:, channels].unsqueeze(2)))
                        dve.wait_ge(rg_done, nth(q))
                        step.add(nc.vector.tensor_tensor(inp, inp, xc[:], ALU.mult))
                        dve.wait_ge(decay_done, nth(q))
                        dve.wait_ge(y_stored, nth_store(q - 1))
                        step(nc.vector.tensor_scalar(y[:], s_, 1.0, None, ALU.add))
                        step(nc.vector.reciprocal(y[:], y[:]))
                        nc.vector.scalar_tensor_tensor(out=s_, in0=s_, scalar=2.0 ** -116, in1=y[:],
                                                       op0=ALU.max, op1=ALU.mult).then_inc(ratio_done, 1)
                        dve.wait_ge(mult_done, nth(q))
                        step(nc.vector.tensor_tensor(inp, inp, s_, ALU.mult))
                        for c in range(LCT):
                            step.add(nc.vector.tensor_tensor_scan(hs[:, c], a[:, c], inp[:, c],
                                                                  h_start[:, c:c + 1], ALU.mult, ALU.add))
                        dve.wait_ge(gate_done, nth(q))
                        step.wait()
                        nc.vector.tensor_tensor(y[:], hs[:], gate[:], ALU.mult).then_inc(y_done, 1)
                        step.add(nc.vector.tensor_copy(last_h[:, channels].unsqueeze(2), hs[:, :, GROUP - 1:]))
                        step.wait()
                        dve.wait_ge(y_done, nth(q))
                    assert step.n == IN_BLOCK, step.n

        @block.tensor
        def _(pe):
            with pe.Fori(0, HALVES) as half:
                for i in range(HT):
                    t = half * HT + i
                    if i == 0:
                        pe.wait_ge(gate_done, nth(half * (LRU_BLOCKS * NG) - 1))
                    pe.wait_ge(hT_lo_done, nth(t - 2))
                    pe.wait_ge(norm.h_done, nth(t))
                    for c in range(KD):
                        last = nc.tensor.transpose(ps[:, 2 * (i % 2) + c // 4, (c % 4) * P:(c % 4 + 1) * P],
                                                   norm.h[:, i % 2, c * P:(c + 1) * P], k.ident[:])
                    last.then_inc(hT_ps_done, 1)
                pe.wait_ge(hT_lo_done, nth(half * HT + (HT - 1)))
                stand(pe)
                with pe.Fori(0, LRU_BLOCKS) as b:
                    n = half * LRU_BLOCKS + b
                    for g in range(NG):
                        q = n * NG + g
                        cols = slice(g * GROUP, (g + 1) * GROUP)

                        def branch(kind, bank, read, done):
                            pe.wait_ge(kind["lo_done"], nth(n))
                            pe.wait_ge(read, nth(q - 1))
                            for o in range(LCT):
                                at = slice(o * P, (o + 1) * P)
                                for c in range(KD):
                                    last = matmul3(nc, ps[:, bank + o], kind["hi"][:, c, at],
                                                   kind["lo"][:, c, at], hT_hi[:, c, cols],
                                                   hT_lo[:, c, cols], c == 0, c == KD - 1)
                            last.then_inc(done, 1)

                        branch(wx, XB, xb_done, xb_ps_done)
                        branch(wg, GB, gate_done, gb_ps_done)
                        pe.wait_ge(wr["lo_done"], nth(n))
                        pe.wait_ge(xc_lo_done, nth(q))
                        pe.wait_ge(rg_done, nth(q - 1))
                        for which, bank in ((0, RG), (1, IG)):
                            for o in range(LCT):
                                at = slice(o * P, (o + 1) * P)
                                for c in range(LCT):
                                    last = matmul3(nc, ps[:, bank + o], wr["hi"][:, which, c, at],
                                                   wr["lo"][:, which, c, at], xc_hi[:, c], xc_lo[:, c],
                                                   c == 0, c == LCT - 1)
                        last.then_inc(rg_ps_done, 1)
        m.end()


def finish(nc, k, x_dram, y_rows, norm_w, out):
    with ExitStack() as ctx:
        m = Memory(nc, ctx, "finish")
        x = m.sb("x", [P, 2, D])
        h = m.sb("h", [P, 2, D])
        square = m.sb("square", [P, D])
        y_a, y_b = m.sb("y_a", [P, 2, D]), m.sb("y_b", [P, 2, D])
        cb = Combine(m, k, x, h, square[:], y_a, y_b)
        stored = [m.store(f"stored{j}") for j in range(2)]
        order = m.plain("vector_order")
        block = m.block()

        @block.sync
        def _(sp):
            m.prime(sp)
            sp.dma_start(cb.norm.norm_w[:], norm_w.partition_broadcast(P)).then_inc(cb.norm.norm_w_in, DMA)
            with sp.Fori(0, NT // 2) as q:
                for j in range(2):
                    t = q * 2 + j
                    sp.wait_ge(cb.norm.h_done, nth(t - 2))
                    sp.dma_start(x[:, j], x_dram[bass.ds(t * P, P), :]).then_inc(cb.x_in[j], DMA)

        @block.gpsimd
        def _(pool):
            with pool.Fori(0, NT // 2) as q:
                for j in range(2):
                    cb.pool(nc, pool, y_rows, j, q * 2 + j, q)

        @block.scalar
        def _(act):
            with act.Fori(0, NT // 2) as q:
                for j in range(2):
                    t = q * 2 + j
                    cb.scalar(nc, act, j, t)
                    act.wait_ge(cb.norm.h_done, nth(t))
                    act.dma_start(out[bass.ds(t * P, P), :], h[:, j]).then_inc(stored[j], DMA)
            for j in range(2):
                act.wait_ge(stored[j], nth_store(NT // 2 - 1))

        @block.vector
        def _(dve):
            step = Steps(dve, order)
            dve.wait_ge(cb.norm.norm_w_in, nth_dma(0))
            with dve.Fori(0, NT // 2) as q:
                step.loop(q * (2 * Combine.STEPS))
                for j in range(2):
                    dve.wait_ge(stored[j], nth_store(q - 1))
                    cb.vector(nc, dve, step, j, q * 2 + j, q)
        m.end()


def build(nc, x, gla_norm, gla_w_in, gla_w_alpha, gla_b_alpha, gla_head_norm, gla_w_out,
          lru_norm, lru_w_in, lru_conv_w, lru_conv_b, lru_w_rgate, lru_b_rgate, lru_w_igate,
          lru_b_igate, lru_lambda, lru_w_out, moe_norm, moe_w_group, moe_w_expert, moe_w_gate,
          moe_w_up, moe_w_down, final_norm, out):
    def scratch(name, shape, dt=F32):
        return nc.dram_tensor(name, shape, dt, kind="Internal").ap()

    oT = scratch("oT_rows", [D, T])
    x1, x2, x3 = (scratch(f"x{n}_rows", [T, D]) for n in (1, 2, 3))
    h_rows = scratch("h_rows", [T, D])
    y_rows = scratch("y_rows", [(MAX_BLOCKS + 1) * P, D])
    ids = scratch("gather_lists", [P * E * SLOTS, 1], I32)
    with ExitStack() as ctx:
        k = Consts(nc, ctx)
        constants(nc, k)
        gla(nc, k, x[0], gla_norm[0], gla_w_in[0], gla_w_alpha[0], gla_b_alpha[0], gla_head_norm[0], oT)
        project_and_route(nc, k, "route0", oT, gla_w_out[0], x[0], x1, h_rows, moe_norm[0],
                          moe_w_group[0], moe_w_expert[0], ids, y_rows[(MIN_BLOCKS + 1) * P:, :])
        experts(nc, k, "experts0", h_rows, ids, moe_w_gate[0], moe_w_up[0], moe_w_down[0], y_rows)
        lru(nc, k, x1, y_rows, x2, lru_norm[0], lru_w_in[0], lru_conv_w[0], lru_conv_b[0],
            lru_w_rgate[0], lru_b_rgate[0], lru_w_igate[0], lru_b_igate[0], lru_lambda[0], oT)
        project_and_route(nc, k, "route1", oT, lru_w_out[0], x2, x3, h_rows, moe_norm[1],
                          moe_w_group[1], moe_w_expert[1], ids)
        experts(nc, k, "experts1", h_rows, ids, moe_w_gate[1], moe_w_up[1], moe_w_down[1], y_rows)
        finish(nc, k, x3, y_rows, final_norm, out[0])


INPUTS = ["x", "gla_norm", "gla_w_in", "gla_w_alpha", "gla_b_alpha", "gla_head_norm", "gla_w_out",
          "lru_norm", "lru_w_in", "lru_conv_w", "lru_conv_b", "lru_w_rgate", "lru_b_rgate",
          "lru_w_igate", "lru_b_igate", "lru_lambda", "lru_w_out", "moe_norm", "moe_w_group",
          "moe_w_expert", "moe_w_gate", "moe_w_up", "moe_w_down", "final_norm"]


def kernel(**inputs):
    import numpy as np
    import concourse.bacc as bacc
    from concourse.bass_utils import run_bass_kernel_spmd

    nc = bacc.Bacc("TRN2", target_bir_lowering=False, num_devices=1)
    arrays, args = {}, []
    for name in INPUTS:
        a = np.ascontiguousarray(inputs[name])
        arrays[f"in_{name}"] = a
        args.append(nc.dram_tensor(f"in_{name}", a.shape, mybir.dt.from_np(a.dtype), kind="ExternalInput").ap())
    out = nc.dram_tensor("out", (1, T, D), F32, kind="ExternalOutput").ap()
    build(nc, *args, out)
    r = run_bass_kernel_spmd(nc, [arrays], core_ids=[0])
    return r.results[0]["out"]
```

```python
import math
from contextlib import ExitStack

import concourse.bass as bass
from concourse import mybir
from concourse.alu_op_type import AluOpType as ALU

ACT = mybir.ActivationFunctionType
AX = mybir.AxisListType
F32 = mybir.dt.float32
F32R = mybir.dt.float32r
BF16 = mybir.dt.bfloat16
I32 = mybir.dt.int32
U32 = mybir.dt.uint32

P = 128
BANK = 512
START = 4
DMA = 16

T = 2048
D = 1024
KD = D // P
NT = T // P
EPS = 1e-6

HALVES = 2
TH = T // HALVES
HT = TH // P
GROUP = 512
NG = TH // GROUP
GT = GROUP // P

HEADS = 4
DK = 128
DV = 256
RANK = 16
CHUNK = 64
NC = GROUP // CHUNK
GATE_TEMP = 16.0

LRU_BLOCKS = 4
LBW = 256
LCT = LBW // P
TAPS = 4
LRU_STEPS = 33
LRU_C = 8.0

GROUPS = 4
EPG = 8
E = GROUPS * EPG
FF = 256
KF = FF // P
SLOTS = T // P
MAX_BLOCKS = 2 * T // P + E
MIN_BLOCKS = E


def nth(k):
    return k + (START + 1)


def nth_dma(k):
    return k * DMA + DMA


def nth_store(k):
    return k * DMA + DMA * (START + 1)


class Steps:

    def __init__(self, eng, sem):
        self.eng, self.sem, self.base, self.n = eng, sem, 0, 0

    def __call__(self, ins):
        self.add(ins)
        self.wait()

    def add(self, ins):
        ins.then_inc(self.sem, 1)
        self.n += 1

    def wait(self):
        self.eng.wait_ge(self.sem, self.base + self.n)

    def loop(self, done):
        self.base, self.n = done, 0

    def after(self, done):
        self.base, self.n = done, 0


def matmul3(nc, out, w_hi, w_lo, x_hi, x_lo, first, last):
    nc.tensor.matmul(out, w_hi, x_hi, start=first, stop=False)
    nc.tensor.matmul(out, w_hi, x_lo, start=False, stop=False)
    return nc.tensor.matmul(out, w_lo, x_hi, start=False, stop=last)


class Memory:

    def __init__(self, nc, ctx, stage):
        self.nc, self.ctx, self.stage = nc, ctx, stage
        self.primed, self.stores, self.held = [], [], []

    def sb(self, name, shape, dt=F32):
        return self.ctx.enter_context(self.nc.sbuf_tensor(f"{self.stage}_{name}", shape, dt))

    def ps(self, name, shape, dt=F32):
        return self.ctx.enter_context(self.nc.psum_tensor(f"{self.stage}_{name}", shape, dt))

    def plain(self, name):
        s = self.nc.alloc_semaphore(name=f"{self.stage}_{name}")
        self.held.append(s)
        return s

    def sem(self, name):
        s = self.plain(name)
        self.primed.append(s)
        return s

    def store(self, name):
        s = self.plain(name)
        self.stores.append(s)
        return s

    def block(self):
        self.block_ctx = ExitStack()
        return self.block_ctx.enter_context(self.nc.Block())

    def end(self):
        self.block_ctx.close()
        self.nc.clear_and_free_semaphores(self.held)
        self.nc.all_engine_barrier()

    def prime(self, sp):
        for s in self.primed:
            sp.sem_inc(s, START)
        for s in self.stores:
            sp.sem_inc(s, START * DMA)


def stand(eng):
    eng.nop(nofuse=True)


class Consts:

    def __init__(self, nc, ctx):
        def sb(name, shape, dt=F32):
            return ctx.enter_context(nc.sbuf_tensor(name, shape, dt))

        self.ident = sb("ident", [P, P])
        self.causal = sb("causal", [P, P])
        self.keep = sb("keep", [P, GROUP])
        self.before = sb("before", [P, P], BF16)
        self.ones_bf = sb("ones_bf", [P, P], BF16)
        self.ones_row = sb("ones_row", [P, E])
        self.token = sb("token", [P, NT], I32)
        self.expert_no = sb("expert_no", [P, E])
        self.eps = sb("eps", [P, 1])
        self.weight = sb("weight", [P, NT, 2])
        self.row = sb("row", [P, NT, 2], I32)
        self.blocks = sb("blocks", [P, E], I32)
        self.block_at = sb("block_at", [P, E], I32)


def constants(nc, k):
    with ExitStack() as ctx:
        made = ctx.enter_context(nc.semaphore("constants_made"))
        block = ctx.enter_context(nc.Block())

        @block.gpsimd
        def _(pool):
            done = Steps(pool, made)
            done.add(pool.memset(k.ident[:], 0.0))
            done.add(pool.memset(k.causal[:], 1.0))
            done.add(pool.memset(k.keep[:], 1.0))
            done.add(pool.memset(k.before[:], 1.0))
            done.add(pool.memset(k.ones_bf[:], 1.0))
            done.add(pool.memset(k.ones_row[:], 1.0))
            done.add(pool.memset(k.eps[:], EPS))
            done.add(pool.iota(k.token[:], [[P, NT]], base=0, channel_multiplier=1))
            done.add(pool.iota(k.expert_no[:], [[1, E]], base=0, channel_multiplier=0,
                               allow_small_or_imprecise_dtypes=True))
            done.wait()
            done.add(pool.affine_select(out=k.ident[:], in_=k.ident[:], compare_op=ALU.not_equal,
                                        fill=1.0, base=0, pattern=[[-1, P]], channel_multiplier=1))
            done.add(pool.affine_select(out=k.causal[:], in_=k.causal[:], compare_op=ALU.is_ge,
                                        fill=0.0, base=0, pattern=[[1, P]], channel_multiplier=-1))
            done.add(pool.affine_select(out=k.before[:], in_=k.before[:], compare_op=ALU.is_gt,
                                        fill=0.0, base=0, pattern=[[1, P]], channel_multiplier=-1))
            chunk_starts = k.keep[:].rearrange("p (c t) -> p c t", t=CHUNK)[:, :, 0]
            done.add(pool.memset(chunk_starts, 0.0))
            done.wait()
            done(pool.memset(k.causal[0:CHUNK, CHUNK:P], 0.0))


class Norm:

    def __init__(self, m, k, x, h, square, depth=2):
        self.x, self.h, self.eps, self.square, self.depth = x, h, k.eps, square, depth
        self.norm_w = m.sb("norm_w", [P, D])
        self.ss = m.sb("ss", [P, depth])
        self.std = m.sb("std", [P, depth])
        self.rstd = m.sb("rstd", [P, depth])
        self.norm_w_in = m.plain("norm_w_in")
        self.ss_done = m.sem("ss_done")
        self.std_done = m.sem("std_done")
        self.h_done = m.sem("h_done")

    def scalar(self, nc, act, j, t):
        act.wait_ge(self.std_done, nth(t - self.depth))
        nc.scalar.activation(self.square, self.x[:, j], ACT.Square, accum_out=self.ss[:, j:j + 1])\
            .then_inc(self.ss_done, 1)
        act.wait_ge(self.h_done, nth(t - self.depth))
        act.wait_ge(self.ss_done, nth(t))
        nc.scalar.activation(self.std[:, j:j + 1], self.ss[:, j:j + 1], ACT.Sqrt,
                             bias=self.eps[:, 0:1], scale=1.0 / D).then_inc(self.std_done, 1)

    def vector(self, nc, dve, step, j, t):
        dve.wait_ge(self.std_done, nth(t))
        step(nc.vector.reciprocal(self.rstd[:, j:j + 1], self.std[:, j:j + 1]))
        nc.vector.scalar_tensor_tensor(out=self.h[:, j], in0=self.x[:, j], scalar=self.rstd[:, j:j + 1],
                                       in1=self.norm_w[:], op0=ALU.mult, op1=ALU.mult)\
            .then_inc(self.h_done, 1)


def gla(nc, k, x_dram, norm_w, w_in, w_alpha, b_alpha, head_norm, oT_dram, y_unused):
    with ExitStack() as ctx:
        m = Memory(nc, ctx, "gla")
        zeros = m.sb("zeros", [P, DV])
        zeros_set, y_zeroed = m.plain("zeros_set"), m.plain("y_zeroed")
        hT_hi = m.sb("hT_hi", [P, KD, TH], F32R)
        hT_lo = m.sb("hT_lo", [P, KD, TH], F32R)
        work = m.sb("work", [P, 4, D])
        q_k = m.sb("q_k", [P, 2 * GROUP])
        q_sb, k_sb = q_k[:, 0:GROUP], q_k[:, GROUP:]
        norm = Norm(m, k, work[:, 0:2], work[:, 2:4], q_k[:, 0:D])
        vg = work[:, 0:2].rearrange("p a (b c) -> p (a b) c", c=2 * DV)
        o_raw = work[:, 2].rearrange("p (a c) -> p a c", c=DV)
        gated = work[:, 3].rearrange("p (a c) -> p a c", c=DV)

        w_raw = m.sb("w_raw", [P, KD * 2 * DV])
        wqk_raw = w_raw[:, 0:KD * 2 * DK].rearrange("p (k c) -> p k c", k=KD)
        wvg_raw = w_raw[:].rearrange("p (k c) -> p k c", k=KD)
        wqk_hi = m.sb("wqk_hi", [P, KD, 2 * DK], F32R)
        wqk_lo = m.sb("wqk_lo", [P, KD, 2 * DK], F32R)
        wvg_hi = m.sb("wvg_hi", [P, KD, 2 * DV], F32R)
        wvg_lo = m.sb("wvg_lo", [P, KD, 2 * DV], F32R)
        wlr_raw = m.sb("wlr_raw", [P, KD, RANK])
        wlr_hi = m.sb("wlr_hi", [P, KD, RANK], F32R)
        wlr_lo = m.sb("wlr_lo", [P, KD, RANK], F32R)
        wal_in, wal = m.sb("w_alpha_in", [RANK, DK]), m.sb("w_alpha", [RANK, DK])
        bal_in, bal = m.sb("b_alpha_in", [P, 1]), m.sb("b_alpha", [P, 1])
        hn = m.sb("head_norm", [P, DV // P])
        lrT = m.sb("lrT", [RANK, TH])

        q_in, k_in, q_x, k_x, q_dec, k_dec = (m.sb(s, [P, NG, GROUP]) for s in (
            "q_in", "k_in", "q_x", "k_x", "q_dec", "k_dec"))
        tile_decay = m.sb("tile_decay", [P, NG, GT])
        z = m.sb("z", [P, GROUP])
        soft = m.sb("soft", [P, GROUP])
        cum = m.sb("cum", [P, GROUP])
        to_mid = soft
        to_end = m.sb("to_end", [P, GROUP])
        e_chunk = m.sb("e_chunk", [P, NC])
        state = m.sb("state", [P, HEADS, DV])
        o_square = m.sb("o_square", [P, DV])
        sT = m.sb("sT", [P, 2, P])
        kd = m.sb("kd", [P, 2, P])
        oss = m.sb("oss", [P, GT])
        ostd = m.sb("ostd", [P, GT])
        orstd = m.sb("orstd", [P, GT])
        oT = m.sb("oT", [P, DV // P, GROUP])

        ps = m.ps("ps", [P, 8, BANK])
        Q, K, LA, VG, SC, O, UP = 0, 1, 2, 3, 5, 6, 7

        x_in = [m.plain(f"x_in{j}") for j in range(2)]
        hT_ps_done, hT_hi_done, hT_lo_done = m.sem("hT_ps_done"), m.sem("hT_hi_done"), m.sem("hT_lo_done")
        small_in = m.plain("small_in")
        wlr_done, zeroed = m.plain("wlr_done"), m.plain("zeroed")
        wqk_in, wvg_in = m.plain("wqk_in"), m.plain("wvg_in")
        wqk_hi_done, wqk_lo_done = m.sem("wqk_hi_done"), m.sem("wqk_lo_done")
        wvg_hi_done, wvg_lo_done = m.sem("wvg_hi_done"), m.sem("wvg_lo_done")
        lr_ps_done, lrT_done = m.sem("lr_ps_done"), m.sem("lrT_done")
        qkz_ps_done = m.sem("qkz_ps_done")
        soft_steps = m.sem("soft_steps")
        cum_done, exps_done, group_done = m.sem("cum_done"), m.sem("exps_done"), m.sem("group_done")
        vg_ps_done, vg_done = m.sem("vg_ps_done"), m.sem("vg_done")
        sc_ps_done, sc_done = m.sem("sc_ps_done"), m.sem("sc_done")
        ou_ps_done = m.sem("ou_ps_done")
        o_raw_done, state_done = m.sem("o_raw_done"), m.sem("state_done")
        oss_done, ostd_done = m.sem("oss_done"), m.sem("ostd_done")
        og_done, oT_ps_done, oT_done = m.sem("og_done"), m.sem("oT_ps_done"), m.sem("oT_done")
        oT_stored = m.store("oT_stored")
        order = m.plain("vector_order")
        block = m.block()

        w_rows = w_in.rearrange("(k p) c -> p k c", p=P)
        KC, VC = HEADS * DK, 2 * HEADS * DK
        GC, LC = VC + D, VC + 2 * D

        @block.sync
        def _(sp):
            m.prime(sp)

            def load_qk(h):
                sp.dma_start(wqk_raw[:, :, 0:DK], w_rows[:, :, bass.ds(h * DK, DK)]).then_inc(wqk_in, DMA)
                sp.dma_start(wqk_raw[:, :, DK:], w_rows[:, :, bass.ds(h * DK + KC, DK)]).then_inc(wqk_in, DMA)
                sp.dma_start(wal_in[:], w_alpha[:, bass.ds(h * DK, DK)]).then_inc(wqk_in, DMA)
                with nc.allow_non_contiguous_dma(reason="128 biases"):
                    sp.dma_start(bal_in[:], b_alpha.rearrange("(c o) -> c o", o=1)[bass.ds(h * DK, DK), :])\
                        .then_inc(wqk_in, DMA)

            def load_vg(h):
                sp.dma_start(wvg_raw[:, :, 0:DV], w_rows[:, :, bass.ds(h * DV + VC, DV)]).then_inc(wvg_in, DMA)
                sp.dma_start(wvg_raw[:, :, DV:], w_rows[:, :, bass.ds(h * DV + GC, DV)]).then_inc(wvg_in, DMA)

            for i in range(2):
                sp.dma_start(norm.x[:, i], x_dram[i * P:(i + 1) * P, :]).then_inc(x_in[i], DMA)
            sp.dma_start(norm.norm_w[:], norm_w.partition_broadcast(P)).then_inc(norm.norm_w_in, DMA)
            sp.dma_start(wlr_raw[:], w_rows[:, :, LC:LC + RANK]).then_inc(small_in, DMA)
            with nc.allow_non_contiguous_dma(reason="256 gains"):
                sp.dma_start(hn[:], head_norm.rearrange("(h p) -> p h", p=P)).then_inc(small_in, DMA)
            load_qk(0)
            sp.wait_ge(wqk_lo_done, nth(0))
            load_vg(0)
            with sp.Fori(0, HALVES) as half:
                for i in range(2, HT):
                    sp.wait_ge(norm.h_done, nth(half * HT + (i - 2)))
                    sp.dma_start(norm.x[:, i % 2], x_dram[bass.ds(half * TH + i * P, P), :])\
                        .then_inc(x_in[i % 2], DMA)
                with sp.Fori(0, HEADS) as h:
                    n = half * HEADS + h
                    sp.wait_ge(wvg_lo_done, nth(n))
                    load_qk((h + 1) % HEADS)
                    sp.wait_ge(wqk_lo_done, nth(n + 1))
                    load_vg((h + 1) % HEADS)
                    for g in range(NG):
                        sp.wait_ge(oT_done, nth(n * NG + g))
                        for e in range(DV // P):
                            sp.dma_start(oT_dram[bass.ds(h * DV + e * P, P),
                                                 bass.ds(half * TH + g * GROUP, GROUP)],
                                         oT[:, e]).then_inc(oT_stored, DMA)
                for i in range(2):
                    sp.dma_start(norm.x[:, i], x_dram[bass.ds(((half + 1) % HALVES) * TH + i * P, P), :])\
                        .then_inc(x_in[i], DMA)
            sp.wait_ge(oT_stored, nth_store(HALVES * HEADS * NG * (DV // P) - 1))
            sp.wait_ge(wqk_in, nth_dma(4 * HALVES * HEADS + 3))
            sp.wait_ge(wvg_in, nth_dma(2 * HALVES * HEADS + 1))
            for i in range(2):
                sp.wait_ge(x_in[i], nth_dma(HALVES * HT // 2))

        @block.gpsimd
        def _(pool):
            pool.memset(zeros[:], 0.0).then_inc(zeros_set, 1)
            pool.wait_ge(zeros_set, 1)
            heads = HALVES * HEADS
            rows = y_unused.shape[0] // heads
            with pool.Fori(0, heads) as n:
                pool.wait_ge(group_done, nth(n * NG))
                stand(pool)
                pool.dma_start(y_unused[bass.ds(n * rows, rows), :]
                               .rearrange("(p n) (a c) -> p (n a) c", p=P, c=DV),
                               zeros[:].unsqueeze(1).to_broadcast([P, rows // P * (D // DV), DV]))\
                    .then_inc(y_zeroed, DMA)
            pool.wait_ge(y_zeroed, nth_dma(heads - 1))

        @block.scalar
        def _(act):
            def split_qk(n):
                act.wait_ge(wqk_in, nth_dma(4 * n + 3))
                nc.scalar.activation(wqk_hi[:], wqk_raw, ACT.Copy).then_inc(wqk_hi_done, 1)

            def square_o(i, t):
                act.wait_ge(oss_done, nth(t - 1))
                act.wait_ge(o_raw_done, nth(t))
                nc.scalar.activation(o_square[:], o_raw[:, i], ACT.Square,
                                     accum_out=oss[:, i:i + 1]).then_inc(oss_done, 1)

            def take_oT(ng, bank):
                act.wait_ge(oT_ps_done, nth(ng))
                act.wait_ge(oT_stored, nth_store(2 * ng - 1))
                for e in range(DV // P):
                    last = nc.scalar.activation(oT[:, e], ps[:, bank + e], ACT.Copy, scale=hn[:, e:e + 1])
                last.then_inc(oT_done, 1)

            act.wait_ge(small_in, nth_dma(1))
            nc.scalar.activation(wlr_hi[:], wlr_raw[:], ACT.Copy).then_inc(wlr_done, 1)
            split_qk(0)
            with act.Fori(0, HALVES) as half:
                def root_mean_square(i):
                    act.wait_ge(x_in[i % 2], nth_dma(half * (HT // 2) + i // 2))
                    norm.scalar(nc, act, i % 2, half * HT + i)

                root_mean_square(0)
                for i in range(HT):
                    t = half * HT + i
                    if i + 1 < HT:
                        root_mean_square(i + 1)
                    act.wait_ge(hT_ps_done, nth(t))
                    for b in range(2):
                        nc.scalar.activation(hT_hi[:, 4 * b:4 * b + 4, i * P:(i + 1) * P],
                                             ps[:, 2 * (i % 2) + b].rearrange("p (a c) -> p a c", c=P),
                                             ACT.Copy).then_inc(hT_hi_done, 1)
                for g in range(NG):
                    act.wait_ge(lr_ps_done, nth(half * NG + g))
                    nc.scalar.activation(lrT[:, g * GROUP:(g + 1) * GROUP], ps[0:RANK, LA], ACT.Copy)\
                        .then_inc(lrT_done, 1)
                with act.Fori(0, HEADS) as h:
                    n = half * HEADS + h
                    act.wait_ge(wvg_in, nth_dma(2 * n + 1))
                    act.wait_ge(vg_ps_done, nth(n * HT - 1))
                    nc.scalar.activation(wvg_hi[:], wvg_raw, ACT.Copy).then_inc(wvg_hi_done, 1)

                    def project(g):
                        ng = n * NG + g
                        act.wait_ge(group_done, nth(ng - 1))
                        act.wait_ge(qkz_ps_done, nth(3 * ng))
                        nc.scalar.activation(q_sb, ps[:, Q], ACT.Copy, scale=DK ** -0.5)
                        act.wait_ge(qkz_ps_done, nth(3 * ng + 1))
                        nc.scalar.activation(k_sb, ps[:, K], ACT.Copy)
                        act.wait_ge(qkz_ps_done, nth(3 * ng + 2))
                        nc.scalar.activation(z[:], ps[:, LA], ACT.Identity, bias=bal[:])\
                            .then_inc(soft_steps, 1)
                        act.wait_ge(soft_steps, nth(4 * ng))
                        nc.scalar.activation(soft[:], z[:], ACT.Abs).then_inc(soft_steps, 1)
                        act.wait_ge(soft_steps, nth(4 * ng + 1))
                        nc.scalar.activation(soft[:], soft[:], ACT.Exp, scale=-1.0).then_inc(soft_steps, 1)
                        act.wait_ge(soft_steps, nth(4 * ng + 2))
                        nc.scalar.activation(soft[:], soft[:], ACT.Ln, bias=1.0).then_inc(soft_steps, 1)

                    def decay(g):
                        ng = n * NG + g
                        act.wait_ge(cum_done, nth(ng))
                        s = 1.0 / GATE_TEMP
                        chunk_ends = cum[:].rearrange("p (c t) -> p c t", t=CHUNK)[:, :, CHUNK - 1]
                        nc.scalar.activation(q_in[:, g], to_mid[:], ACT.Exp, scale=s)
                        nc.scalar.activation(k_in[:, g], to_mid[:], ACT.Exp, scale=-s)
                        nc.scalar.activation(k_x[:, g], to_end[:], ACT.Exp, scale=s)
                        nc.scalar.activation(q_x[:, g], cum[:], ACT.Exp, scale=s)
                        nc.scalar.activation(e_chunk[:], chunk_ends, ACT.Exp, scale=s).then_inc(exps_done, 1)

                    def root(at):
                        nc.scalar.activation(ostd[:, at], oss[:, at], ACT.Sqrt, bias=k.eps[:, 0:1], scale=1.0 / DV)\
                            .then_inc(ostd_done, 1)

                    for g in range(NG):
                        project(g)
                        decay(g)
                    for g in range(NG):
                        ng = n * NG + g
                        for i in range(GT):
                            t = n * HT + g * GT + i
                            if i == 0:
                                act.wait_ge(ostd_done, nth(2 * ng - 2))
                            act.wait_ge(vg_ps_done, nth(t))
                            nc.scalar.activation(vg[:, i], ps[:, VG + i % 2], ACT.Copy).then_inc(vg_done, 1)
                            if i == GT - 1:
                                act.wait_ge(vg_done, nth(t))
                                nc.scalar.activation(gated[:, i], vg[:, i, DV:], ACT.Silu)
                            if g or i:
                                square_o((i - 1) % GT, t - 1)
                            if g and i == 0:
                                act.wait_ge(oss_done, nth(t - 1))
                                root(slice(GT - 1, GT))
                            if g == 0 and i == 1:
                                split_qk(n + 1)
                            if g and i == 2:
                                take_oT(ng - 1, Q)
                            if i == GT - 2:
                                act.wait_ge(vg_done, nth(t))
                                nc.scalar.activation(gated[:, 0:GT - 1], vg[:, 0:GT - 1, DV:], ACT.Silu)
                        act.wait_ge(oss_done, nth(t - 1))
                        act.wait_ge(ostd_done, nth(2 * ng - 1))
                        root(slice(0, GT - 1))
                    square_o(GT - 1, t)
                    act.wait_ge(oss_done, nth(t))
                    root(slice(GT - 1, GT))
                    take_oT(ng, VG)

        STEPS_PER_HEAD = 14
        STEPS_PER_HALF = HT + HEADS * STEPS_PER_HEAD

        @block.vector
        def _(dve):
            step = Steps(dve, order)
            nc.vector.memset(sT[:], 0.0)
            nc.vector.memset(state[:], 0.0).then_inc(zeroed, 1)
            dve.wait_ge(zeroed, 1)
            dve.wait_ge(wlr_done, 1)
            nc.vector.tensor_tensor(wlr_lo[:], wlr_raw[:], wlr_hi[:].bitcast(F32), ALU.subtract)\
                .then_inc(wlr_done, 1)
            dve.wait_ge(norm.norm_w_in, nth_dma(0))

            def split_qk(n):
                dve.wait_ge(wqk_hi_done, nth(n))
                nc.vector.tensor_copy(wal[:], wal_in[:])
                nc.vector.tensor_copy(bal[:], bal_in[:])
                nc.vector.tensor_tensor(wqk_lo[:], wqk_raw, wqk_hi[:].bitcast(F32), ALU.subtract)\
                    .then_inc(wqk_lo_done, 1)

            def chunks(x):
                return x.rearrange("p (c t) -> p c t", t=CHUNK)

            def two_chunks(x):
                return x.rearrange("p (a b t) -> p a b t", b=2, t=CHUNK)

            split_qk(0)
            with dve.Fori(0, HALVES) as half:
                step.loop(half * STEPS_PER_HALF)
                def normalise(i):
                    t = half * HT + i
                    dve.wait_ge(hT_ps_done, nth(t - 2))
                    norm.vector(nc, dve, step, i % 2, t)

                normalise(0)
                for i in range(HT):
                    t = half * HT + i
                    if i + 1 < HT:
                        normalise(i + 1)
                    for b in range(2):
                        dve.wait_ge(hT_hi_done, nth(2 * t + b))
                        part = (slice(None), slice(4 * b, 4 * b + 4), slice(i * P, (i + 1) * P))
                        last = nc.vector.tensor_tensor(
                            hT_lo[part], ps[:, 2 * (i % 2) + b].rearrange("p (a c) -> p a c", c=P),
                            hT_hi[part].bitcast(F32), ALU.subtract)
                    last.then_inc(hT_lo_done, 1)
                with dve.Fori(0, HEADS) as h:
                    n = half * HEADS + h
                    step.loop(half * STEPS_PER_HALF + h * STEPS_PER_HEAD + HT)
                    dve.wait_ge(wvg_hi_done, nth(n))
                    nc.vector.tensor_tensor(wvg_lo[:], wvg_raw, wvg_hi[:].bitcast(F32), ALU.subtract)\
                        .then_inc(wvg_lo_done, 1)

                    def sum_up(g):
                        ng = n * NG + g
                        dve.wait_ge(soft_steps, nth(4 * ng + 3))
                        step(nc.vector.tensor_scalar(z[:], z[:], 0.0, None, ALU.min))
                        step(nc.vector.tensor_tensor(z[:], z[:], soft[:], ALU.subtract))
                        step(nc.vector.tensor_tensor_scan(cum[:], k.keep[:], z[:], 0.0, ALU.mult, ALU.add))
                        c = chunks(cum[:])
                        mid = c[:, :, CHUNK // 2:CHUNK // 2 + 1].to_broadcast([P, NC, CHUNK])
                        end = c[:, :, CHUNK - 1:CHUNK].to_broadcast([P, NC, CHUNK])
                        nc.vector.tensor_tensor(chunks(to_mid[:]), c, mid, ALU.subtract)
                        nc.vector.tensor_tensor(chunks(to_end[:]), end, c, ALU.subtract).then_inc(cum_done, 1)

                    def decay(g):
                        dve.wait_ge(exps_done, nth(n * NG + g))
                        step.add(nc.vector.tensor_tensor(k_x[:, g], k_x[:, g], k_sb, ALU.mult))
                        step.add(nc.vector.tensor_tensor(q_x[:, g], q_x[:, g], q_sb, ALU.mult))
                        nc.vector.tensor_tensor(q_in[:, g], q_in[:, g], q_sb, ALU.mult)
                        nc.vector.tensor_tensor(k_in[:, g], k_in[:, g], k_sb, ALU.mult)
                        step.wait()
                        of_pair = e_chunk[:].rearrange("p (a b) -> p a b", b=2)
                        qx, kx = two_chunks(q_x[:, g]), two_chunks(k_x[:, g])
                        qd, kdec = two_chunks(q_dec[:, g]), two_chunks(k_dec[:, g])
                        nc.vector.tensor_copy(qd[:, :, 0], qx[:, :, 0])
                        nc.vector.tensor_tensor(qd[:, :, 1], qx[:, :, 1],
                                                of_pair[:, :, 0:1].to_broadcast([P, GT, CHUNK]), ALU.mult)
                        nc.vector.tensor_tensor(kdec[:, :, 0], kx[:, :, 0],
                                                of_pair[:, :, 1:2].to_broadcast([P, GT, CHUNK]), ALU.mult)
                        nc.vector.tensor_copy(kdec[:, :, 1], kx[:, :, 1])
                        nc.vector.tensor_tensor(tile_decay[:, g], of_pair[:, :, 0], of_pair[:, :, 1],
                                                ALU.mult).then_inc(group_done, 1)

                    def take_scores(i, t):
                        dve.wait_ge(ou_ps_done, nth(2 * t - 3))
                        dve.wait_ge(sc_ps_done, nth(t))
                        nc.vector.tensor_copy(kd[:, i % 2], ps[:, SC, 192:320])
                        for c in range(2):
                            own, at = slice(c * CHUNK, (c + 1) * CHUNK), slice(c * CHUNK, (c + 1) * CHUNK)
                            nc.vector.copy_predicated(sT[own, i % 2, at], k.causal[own, at].bitcast(U32),
                                                      ps[own, SC, at])
                        nc.vector.tensor_copy(sT[0:CHUNK, i % 2, CHUNK:P], ps[0:CHUNK, SC, P:P + CHUNK])\
                            .then_inc(sc_done, 1)

                    def take_outputs(i, t, g):
                        dve.wait_ge(ou_ps_done, nth(2 * t))
                        nc.vector.tensor_copy(o_raw[:, i], ps[:, O, 0:DV]).then_inc(o_raw_done, 1)
                        dve.wait_ge(ou_ps_done, nth(2 * t + 1))
                        nc.vector.scalar_tensor_tensor(
                            out=state[:, bass.ds(h, 1)], in0=state[:, bass.ds(h, 1)],
                            scalar=tile_decay[:, g, i:i + 1], in1=ps[:, UP, 0:DV].unsqueeze(1),
                            op0=ALU.mult, op1=ALU.add).then_inc(state_done, 1)

                    def gate_outputs(tiles, roots):
                        dve.wait_ge(ostd_done, nth(roots))
                        step(nc.vector.reciprocal(orstd[:, tiles[0]:tiles[-1] + 1], ostd[:, tiles[0]:tiles[-1] + 1]))
                        for i in tiles:
                            last = nc.vector.scalar_tensor_tensor(
                                out=gated[:, i], in0=o_raw[:, i], scalar=orstd[:, i:i + 1],
                                in1=gated[:, i], op0=ALU.mult, op1=ALU.mult)
                        last.then_inc(og_done, 1)

                    sum_up(0)
                    decay(0)
                    sum_up(1)
                    for g in range(NG):
                        ng = n * NG + g
                        for i in range(GT):
                            t = n * HT + g * GT + i
                            take_scores(i, t)
                            if g or i:
                                take_outputs((i - 1) % GT, t - 1, g if i else g - 1)
                            if g == 0 and i == 0:
                                decay(1)
                            if g == 0 and i == 1:
                                split_qk(n + 1)
                            if g and i == 0:
                                gate_outputs([GT - 1], 2 * ng - 1)
                        if g == NG - 1:
                            take_outputs(GT - 1, t, g)
                        gate_outputs(range(GT - 1), 2 * ng)
                    gate_outputs([GT - 1], 2 * ng + 1)
                    assert step.n == STEPS_PER_HEAD, step.n

        @block.tensor
        def _(pe):
            def transpose_outputs(tiles, bank):
                for e in range(DV // P):
                    for i in tiles:
                        last = nc.tensor.transpose(ps[:, bank + e, i * P:(i + 1) * P],
                                                   gated[:, i, e * P:(e + 1) * P], k.ident[:])
                return last

            pe.wait_ge(wlr_done, 2)
            pe.wait_ge(zeroed, 1)
            with pe.Fori(0, HALVES) as half:
                pe.wait_ge(oT_done, nth(half * (HEADS * NG) - 1))
                for i in range(HT):
                    t = half * HT + i
                    pe.wait_ge(hT_lo_done, nth(t - 2))
                    pe.wait_ge(norm.h_done, nth(t))
                    for c in range(KD):
                        last = nc.tensor.transpose(ps[:, 2 * (i % 2) + c // 4, (c % 4) * P:(c % 4 + 1) * P],
                                                   norm.h[:, i % 2, c * P:(c + 1) * P], k.ident[:])
                    last.then_inc(hT_ps_done, 1)
                pe.wait_ge(hT_lo_done, nth(half * HT + (HT - 1)))
                for g in range(NG):
                    pe.wait_ge(lrT_done, nth(half * NG + (g - 1)))
                    for c in range(KD):
                        cols = slice(g * GROUP, (g + 1) * GROUP)
                        last = matmul3(nc, ps[0:RANK, LA], wlr_hi[:, c], wlr_lo[:, c],
                                       hT_hi[:, c, cols], hT_lo[:, c, cols], c == 0, c == KD - 1)
                    last.then_inc(lr_ps_done, 1)
                pe.wait_ge(lrT_done, nth(half * NG + (NG - 1)))
                stand(pe)
                with pe.Fori(0, HEADS) as h:
                    n = half * HEADS + h
                    pe.wait_ge(oT_done, nth(n * NG - 2))
                    pe.wait_ge(soft_steps, nth(4 * n * NG - 4))
                    pe.wait_ge(wqk_lo_done, nth(n))
                    for g in range(NG):
                        ng = n * NG + g
                        cols = slice(g * GROUP, (g + 1) * GROUP)
                        if g:
                            pe.wait_ge(soft_steps, nth(4 * (ng - 1)))
                        for bank, at in ((Q, 0), (K, DK)):
                            for c in range(KD):
                                last = matmul3(nc, ps[:, bank], wqk_hi[:, c, at:at + DK],
                                               wqk_lo[:, c, at:at + DK], hT_hi[:, c, cols],
                                               hT_lo[:, c, cols], c == 0, c == KD - 1)
                            last.then_inc(qkz_ps_done, 1)
                        nc.tensor.matmul(ps[:, LA], wal[:], lrT[:, cols], start=True, stop=True)\
                            .then_inc(qkz_ps_done, 1)
                    pe.wait_ge(wvg_lo_done, nth(n))

                    def tile_outputs(i, t, g):
                        at = slice(i * P, (i + 1) * P)
                        values = vg[:, i, 0:DV]
                        pe.wait_ge(sc_done, nth(t))
                        pe.wait_ge(vg_done, nth(t))
                        pe.wait_ge(o_raw_done, nth(t - 1))
                        pe.wait_ge(state_done, nth(t - 1))
                        nc.tensor.matmul(ps[:, O, 0:DV], sT[:, i % 2], values, start=True, stop=False)
                        nc.tensor.matmul(ps[:, O, 0:DV], q_dec[:, g, at], state[:, bass.ds(h, 1)],
                                         start=False, stop=True).then_inc(ou_ps_done, 1)
                        nc.tensor.matmul(ps[:, UP, 0:DV], kd[:, i % 2], values, start=True, stop=True)\
                            .then_inc(ou_ps_done, 1)

                    for g in range(NG):
                        ng = n * NG + g
                        for i in range(GT):
                            t = n * HT + g * GT + i
                            at = slice(i * P, (i + 1) * P)
                            tok = slice(g * GROUP + i * P, g * GROUP + (i + 1) * P)
                            if g == 0 and i == 0:
                                pe.wait_ge(oT_done, nth(ng - 1))
                            pe.wait_ge(vg_done, nth(t - 2))
                            for c in range(KD):
                                last = matmul3(nc, ps[:, VG + i % 2], hT_hi[:, c, tok], hT_lo[:, c, tok],
                                               wvg_hi[:, c], wvg_lo[:, c], c == 0, c == KD - 1)
                            last.then_inc(vg_ps_done, 1)
                            pe.wait_ge(group_done, nth(ng))
                            pe.wait_ge(sc_done, nth(t - 1))
                            later = slice(i * P + CHUNK, (i + 1) * P)
                            nc.tensor.matmul(ps[:, SC, 0:P], k_in[:, g, at], q_in[:, g, at],
                                             start=True, stop=True)
                            nc.tensor.matmul(ps[:, SC, P:P + CHUNK], k_x[:, g, at], q_x[:, g, later],
                                             start=True, stop=True)
                            nc.tensor.transpose(ps[:, SC, 192:320], k_dec[:, g, at], k.ident[:])\
                                .then_inc(sc_ps_done, 1)
                            if g or i:
                                tile_outputs((i - 1) % GT, t - 1, g if i else g - 1)
                            if g and i == 1:
                                pe.wait_ge(og_done, nth(2 * ng - 1))
                                transpose_outputs(range(GT), Q).then_inc(oT_ps_done, 1)
                    tile_outputs(GT - 1, t, g)
                    pe.wait_ge(og_done, nth(2 * ng + 1))
                    transpose_outputs(range(GT), VG).then_inc(oT_ps_done, 1)
        m.end()


def project_and_route(nc, k, stage, yT_dram, w_out, x_dram, x_out, h_out, norm_w, w_group, w_expert,
                      ids_out):
    W = GROUPS + E
    with ExitStack() as ctx:
        m = Memory(nc, ctx, stage)
        PARTS = 4
        w_raw = m.sb("w_raw", [P, PARTS, KD // PARTS, D])
        w_hi = m.sb("w_hi", [P, KD, D], F32R)
        w_lo = m.sb("w_lo", [P, KD, D], F32R)
        w_route = m.sb("w_route", [P, KD, W])
        src = m.sb("src", [P, 2, KD, P])
        src_hi = m.sb("src_hi", [P, 2, KD, P], F32R)
        src_lo = m.sb("src_lo", [P, 2, KD, P], F32R)
        x_old = m.sb("x_old", [P, 2, D])
        x_new = m.sb("x_new", [P, 2, D])
        h = m.sb("h", [P, 2, D])
        square = m.sb("square", [P, D])
        norm = Norm(m, k, x_new, h, square[:])
        hT = m.sb("hT", [P, KD, P])
        groups8 = m.sb("groups8", [P, 8])
        experts = m.sb("experts", [P, GROUPS, EPG])
        top_g, top_e = m.sb("top_g", [P, 8]), m.sb("top_e", [P, 8])
        at_g, at_e = m.sb("at_g", [P, 8], U32), m.sb("at_e", [P, 8], U32)
        g_no, e_no = m.sb("g_no", [P, 1]), m.sb("e_no", [P, 2])
        g_first = m.sb("g_first", [P, 1])
        minus_max = m.sb("minus_max", [P, 1])
        behind = m.sb("behind", [P, 1])
        g_exps, g_sum, e_exp = m.sb("g_exps", [P, GROUPS]), m.sb("g_sum", [P, 1]), m.sb("e_exp", [P, 1])
        denom = m.sb("denom", [P, 1])
        g_hot = m.sb("g_hot", [P, GROUPS])
        masked = m.sb("masked", [P, GROUPS, EPG])
        mine = m.sb("mine", [P, EPG])
        hot = m.sb("hot", [P, NT, 2, E])
        both = m.sb("both", [P, E], BF16)
        total = m.sb("total", [P, E])
        ranks = m.sb("ranks", [P, E])
        at_rank = m.sb("at_rank", [P, 2, E])
        rank = m.sb("rank", [P, NT, 2])
        rank_now = m.sb("rank_now", [P, 2])
        rank_int, blk_int = m.sb("rank_int", [P, 2], I32), m.sb("blk_int", [P, 2], I32)
        blk = m.sb("blk", [P, 2])
        place = m.sb("place", [P, 2])
        place_int = m.sb("place_int", [P, 2, 2], I32)
        tok = m.sb("tok", [P, 2], I32)
        zero_ids = m.sb("zero_ids", [P, E * SLOTS], I32)
        nblk, upto = m.sb("nblk", [P, E]), m.sb("upto", [P, E])
        first_row = m.sb("first_row", [P, E])
        spread, start_row = m.sb("spread", [P, NT * 2, E]), m.sb("start_row", [P, NT * 2])

        ps = m.ps("ps", [P, 8, BANK])
        HT_, LG, RK = 4, 6, 7

        w_in = [m.plain(f"w_in{a}") for a in range(PARTS)]
        route_in, zeroed, ids_zero = m.plain("route_in"), m.plain("zeroed"), m.plain("ids_zero")
        w_hi_done, w_lo_done = m.plain("w_hi_done"), m.sem("w_lo_done")
        src_in = [m.plain(f"src_in{j}") for j in range(2)]
        x_in = [m.plain(f"x_in{j}") for j in range(2)]
        src_hi_done, src_lo_done = m.sem("src_hi_done"), m.sem("src_lo_done")
        proj_done, x_done = m.sem("proj_done"), m.sem("x_done")
        x_stored = [m.store(f"x_stored{j}") for j in range(2)]
        h_stored = [m.store(f"h_stored{j}") for j in range(2)]
        scattered = [m.plain(f"scattered{j}") for j in range(2)]
        hT_ps_done, hT_done, logits_done = m.sem("hT_ps_done"), m.sem("hT_done"), m.sem("logits_done")
        maxima_done, exps_done = m.sem("maxima_done"), m.sem("exps_done")
        chosen_done, rank_ps_done, place_done = m.sem("chosen_done"), m.sem("rank_ps_done"), m.sem("place_done")
        order = m.plain("vector_order")
        block = m.block()

        yT = yT_dram.rearrange("(k p) t -> p k t", p=P)
        w_rows = w_out.rearrange("(a b p) c -> a p b c", b=KD // PARTS, p=P)

        def of_part(a):
            return slice(a * (KD // PARTS), (a + 1) * (KD // PARTS))

        def tiles(eng, body):
            for t in range(2):
                body(t, t)
            with eng.Fori(0, NT // 2 - 2) as q:
                for j in range(2):
                    body(q * 2 + (2 + j), j)
            for t in range(NT - 2, NT):
                body(t, t % 2)

        @block.sync
        def _(sp):
            m.prime(sp)
            for t in range(2):
                sp.dma_start(src[:, t], yT[:, :, t * P:(t + 1) * P]).then_inc(src_in[t], DMA)
                for a in range(PARTS if t == 0 else 0):
                    sp.dma_start(w_raw[:, a], w_rows[a]).then_inc(w_in[a], DMA)
                sp.dma_start(x_old[:, t], x_dram[t * P:(t + 1) * P, :]).then_inc(x_in[t], DMA)
            sp.dma_start(norm.norm_w[:], norm_w.partition_broadcast(P)).then_inc(norm.norm_w_in, DMA)
            with nc.allow_non_contiguous_dma(reason="16-byte rows of the group router"):
                sp.dma_start(w_route[:, :, 0:GROUPS], w_group.rearrange("(k p) c -> p k c", p=P))\
                    .then_inc(route_in, DMA)
            sp.dma_start(w_route[:, :, GROUPS:], w_expert.rearrange("(k p) c -> p k c", p=P))\
                .then_inc(route_in, DMA)

            def body(t, j):
                more = not (isinstance(t, int) and t >= NT - 2)
                if more:
                    sp.wait_ge(src_lo_done, nth(t))
                    sp.dma_start(src[:, j], yT[:, :, bass.ds(t * P + 2 * P, P)]).then_inc(src_in[j], DMA)
                sp.wait_ge(x_done, nth(t))
                sp.dma_start(x_out[bass.ds(t * P, P), :], x_new[:, j]).then_inc(x_stored[j], DMA)
                if more:
                    sp.dma_start(x_old[:, j], x_dram[bass.ds(t * P + 2 * P, P), :]).then_inc(x_in[j], DMA)
                sp.wait_ge(norm.h_done, nth(t))
                sp.dma_start(h_out[bass.ds(t * P, P), :], h[:, j]).then_inc(h_stored[j], DMA)

            tiles(sp, body)
            for j in range(2):
                sp.wait_ge(x_stored[j], nth_store(NT // 2 - 1))
                sp.wait_ge(h_stored[j], nth_store(NT // 2 - 1))

        @block.gpsimd
        def _(pool):
            pool.memset(zero_ids[:], 0).then_inc(zeroed, 1)
            pool.wait_ge(zeroed, 1)
            ids = ids_out.rearrange("(p n) o -> p (n o)", p=P)
            pool.dma_start(ids, zero_ids[:]).then_inc(ids_zero, DMA)
            pool.wait_ge(ids_zero, nth_dma(0))

            def body(t, j):
                pool.wait_ge(place_done, nth(t))
                if not isinstance(t, int):
                    stand(pool)
                for c in range(2):
                    pool.indirect_dma_start(
                        ids_out, bass.IndirectOffsetOnAxis(place_int[:, j, c:c + 1].bitcast(U32), 0),
                        tok[:, j:j + 1], None).then_inc(scattered[j], DMA)

            tiles(pool, body)
            for j in range(2):
                pool.wait_ge(scattered[j], NT * DMA)

        @block.scalar
        def _(act):
            def split(t, j, loaded):
                act.wait_ge(src_in[j], nth_dma(loaded))
                act.wait_ge(proj_done, nth(t - 2))
                nc.scalar.activation(src_hi[:, j], src[:, j], ACT.Copy).then_inc(src_hi_done, 1)

            def exps(t):
                act.wait_ge(maxima_done, nth(t))
                nc.scalar.activation(g_exps[:], groups8[:, 0:GROUPS], ACT.Exp, bias=minus_max[:],
                                     accum_out=g_sum[:])
                nc.scalar.activation(e_exp[:], behind[:], ACT.Exp).then_inc(exps_done, 1)

            split(0, 0, 0)
            for a in range(PARTS):
                act.wait_ge(w_in[a], nth_dma(0))
                nc.scalar.activation(w_hi[:, of_part(a)], w_raw[:, a], ACT.Copy).then_inc(w_hi_done, 1)
            split(1, 1, 0)

            def body(t, j):
                act.wait_ge(x_done, nth(t))
                norm.scalar(nc, act, j, t)
                if not (isinstance(t, int) and t >= NT - 2):
                    split(t + 2, j, (t - j) // 2 + 1)
                act.wait_ge(hT_ps_done, nth(t))
                act.wait_ge(logits_done, nth(t - 1))
                for b in range(2):
                    last = nc.scalar.activation(hT[:, 4 * b:4 * b + 4],
                                                ps[:, HT_ + b].rearrange("p (a c) -> p a c", c=P), ACT.Copy)
                last.then_inc(hT_done, 1)
                if not (isinstance(t, int) and t == 0):
                    exps(t - 1)

            tiles(act, body)
            exps(NT - 1)

        @block.vector
        def _(dve):
            step = Steps(dve, order)
            step.add(nc.vector.memset(groups8[:], -3.0e38))
            step.add(nc.vector.memset(total[:], 0.0))
            step.wait()

            def split(t, j):
                dve.wait_ge(src_hi_done, nth(t))
                nc.vector.tensor_tensor(src_lo[:, j], src[:, j], src_hi[:, j].bitcast(F32), ALU.subtract)\
                    .then_inc(src_lo_done, 1)

            split(0, 0)
            for a in range(PARTS):
                dve.wait_ge(w_hi_done, a + 1)
                nc.vector.tensor_tensor(w_lo[:, of_part(a)], w_raw[:, a], w_hi[:, of_part(a)].bitcast(F32),
                                        ALU.subtract).then_inc(w_lo_done, 1)
            split(1, 1)
            dve.wait_ge(norm.norm_w_in, nth_dma(0))

            def choose(t):
                dve.wait_ge(logits_done, nth(t))
                step.add(nc.vector.tensor_copy(groups8[:, 0:GROUPS], ps[:, LG, 0:GROUPS]))
                nc.vector.tensor_copy(experts[:].rearrange("p g e -> p (g e)"), ps[:, LG, GROUPS:W])
                step.wait()
                stand(dve)
                step(nc.vector.max(top_g[:], groups8[:]))
                step.add(nc.vector.tensor_scalar(minus_max[:], top_g[:, 0:1], -1.0, None, ALU.mult))
                stand(dve)
                step(nc.vector.max_index(at_g[:], top_g[:], groups8[:]))
                step(nc.vector.tensor_copy(g_no[:], at_g[:, 0:1]))
                step.add(nc.vector.tensor_scalar(g_first[:], g_no[:], float(EPG), None, ALU.mult))
                step(nc.vector.tensor_scalar(g_hot[:], k.expert_no[:, 0:GROUPS], g_no[:], None, ALU.is_equal))
                step(nc.vector.tensor_tensor(masked[:], experts[:],
                                             g_hot[:].unsqueeze(2).to_broadcast([P, GROUPS, EPG]), ALU.mult))
                step(nc.vector.tensor_reduce(mine[:], masked[:].rearrange("p g e -> p e g"), AX.X, ALU.add))
                stand(dve)
                step(nc.vector.max(top_e[:], mine[:]))
                nc.vector.tensor_tensor(behind[:], top_e[:, 1:2], top_e[:, 0:1], ALU.subtract)\
                    .then_inc(maxima_done, 1)
                step(nc.vector.max_index(at_e[:], top_e[:], mine[:]))
                step(nc.vector.tensor_copy(e_no[:], at_e[:, 0:2]))
                step(nc.vector.tensor_scalar(e_no[:], e_no[:], g_first[:], None, ALU.add))
                for c in range(2):
                    step.add(nc.vector.tensor_scalar(hot[:, bass.ds(t, 1), c], k.expert_no[:].unsqueeze(1),
                                                     e_no[:, c:c + 1], None, ALU.is_equal))
                step.wait()
                nc.vector.tensor_tensor(both[:].unsqueeze(1), hot[:, bass.ds(t, 1), 0],
                                        hot[:, bass.ds(t, 1), 1], ALU.add).then_inc(chosen_done, 1)

            CHOOSE = 15

            def place_tokens(t, j):
                dve.wait_ge(exps_done, nth(t))
                step(nc.vector.tensor_scalar(denom[:], e_exp[:], 1.0, g_sum[:], ALU.add, ALU.mult))
                step(nc.vector.reciprocal(denom[:], denom[:]))
                nc.vector.tensor_copy(k.weight[:, bass.ds(t, 1), 0], denom[:])
                nc.vector.tensor_tensor(k.weight[:, bass.ds(t, 1), 1], denom[:], e_exp[:], ALU.mult)
                dve.wait_ge(rank_ps_done, nth(t))
                step(nc.vector.tensor_tensor(ranks[:], ps[:, RK, 0:E], total[:], ALU.add))
                step.add(nc.vector.tensor_tensor(total[:], ps[:, RK, E:2 * E], total[:], ALU.add))
                step(nc.vector.tensor_tensor(at_rank[:].unsqueeze(1), hot[:, bass.ds(t, 1)],
                                             ranks[:].unsqueeze(1).unsqueeze(1).to_broadcast([P, 1, 2, E]),
                                             ALU.mult))
                step(nc.vector.tensor_reduce(rank_now[:], at_rank[:], AX.X, ALU.add))
                step.add(nc.vector.tensor_copy(rank[:, bass.ds(t, 1)], rank_now[:].unsqueeze(1)))
                step(nc.vector.tensor_copy(rank_int[:], rank_now[:]))
                step(nc.vector.tensor_scalar(blk_int[:], rank_int[:], 7, None, ALU.logical_shift_right))
                step(nc.vector.tensor_copy(blk[:], blk_int[:]))
                step(nc.vector.tensor_scalar(place[:], rank_now[:], float(E * SLOTS), None, ALU.mult))
                step(nc.vector.scalar_tensor_tensor(out=place[:], in0=blk[:], scalar=1.0 - P * E * SLOTS,
                                                    in1=place[:], op0=ALU.mult, op1=ALU.add))
                step(nc.vector.tensor_tensor(at_rank[:].unsqueeze(1), hot[:, bass.ds(t, 1)],
                                             k.expert_no[:].unsqueeze(1).unsqueeze(1)
                                             .to_broadcast([P, 1, 2, E]), ALU.mult))
                step(nc.vector.tensor_reduce(rank_now[:], at_rank[:], AX.X, ALU.add))
                step(nc.vector.scalar_tensor_tensor(out=place[:], in0=rank_now[:], scalar=float(SLOTS),
                                                    in1=place[:], op0=ALU.mult, op1=ALU.add))
                if not (isinstance(t, int) and t < 2):
                    dve.wait_ge(scattered[j], (t - j) * DMA)
                nc.vector.tensor_copy(tok[:, j:j + 1], k.token[:, bass.ds(t, 1)])
                nc.vector.tensor_copy(place_int[:, j], place[:]).then_inc(place_done, 1)

            PLACE = 15
            first = step.n

            def counted(t):
                if isinstance(t, int) and t < 2:
                    return first + 0 if t == 0 else first + 1
                return t * (1 + CHOOSE + PLACE) + (first + 2 + CHOOSE - 2 * (1 + CHOOSE + PLACE))

            def body(t, j):
                step.loop(counted(t))
                dve.wait_ge(proj_done, nth(t))
                dve.wait_ge(x_in[j], nth_dma((t - j) // 2))
                dve.wait_ge(x_stored[j], nth_store((t - j) // 2 - 1))
                dve.wait_ge(norm.h_done, nth(t - 2))
                nc.vector.tensor_tensor(x_new[:, j].rearrange("p (b c) -> p b c", b=2),
                                        ps[:, 2 * j:2 * j + 2],
                                        x_old[:, j].rearrange("p (b c) -> p b c", b=2), ALU.add)\
                    .then_inc(x_done, 1)
                dve.wait_ge(x_done, nth(t))
                dve.wait_ge(h_stored[j], nth_store((t - j) // 2 - 1))
                dve.wait_ge(hT_ps_done, nth(t - 2))
                norm.vector(nc, dve, step, j, t)
                static = isinstance(t, int)
                if not (static and t >= NT - 2):
                    split(t + 2, j)
                if not (static and t < 2):
                    place_tokens(t - 2, j)
                if not (static and t < 1):
                    choose(t - 1)

            tiles(dve, body)
            place_tokens(NT - 2, 0)
            choose(NT - 1)
            place_tokens(NT - 1, 1)
            step(nc.vector.tensor_scalar(nblk[:], total[:], float(P - 1), None, ALU.add))
            step(nc.vector.tensor_copy(k.blocks[:], nblk[:]))
            step(nc.vector.tensor_scalar(k.block_at[:], k.blocks[:], 7, None, ALU.logical_shift_right))
            step(nc.vector.tensor_copy(nblk[:], k.block_at[:]))
            step(nc.vector.tensor_scalar(nblk[:], nblk[:], 1.0, None, ALU.max))
            step(nc.vector.tensor_tensor_scan(upto[:], k.ones_row[:], nblk[:], 0.0, ALU.mult, ALU.add))
            step(nc.vector.tensor_tensor(upto[:], upto[:], nblk[:], ALU.subtract))
            step.add(nc.vector.tensor_copy(k.blocks[:], nblk[:]))
            step.add(nc.vector.tensor_copy(k.block_at[:], upto[:]))
            step(nc.vector.tensor_scalar(first_row[:], upto[:], 1.0, float(P), ALU.add, ALU.mult))
            step(nc.vector.tensor_tensor(spread[:], hot[:].rearrange("p t c e -> p (t c) e"),
                                         first_row[:].unsqueeze(1).to_broadcast([P, NT * 2, E]), ALU.mult))
            step(nc.vector.tensor_reduce(start_row[:], spread[:], AX.X, ALU.add))
            step(nc.vector.tensor_tensor(rank[:].rearrange("p t c -> p (t c)"), start_row[:],
                                         rank[:].rearrange("p t c -> p (t c)"), ALU.add))
            step(nc.vector.tensor_copy(k.row[:], rank[:]))

        @block.tensor
        def _(pe):
            def project(t, j, half):
                if half == 0:
                    pe.wait_ge(src_lo_done, nth(t))
                    pe.wait_ge(x_done, nth(t - 2))
                for c in range(KD):
                    last = matmul3(nc, ps[:, 2 * j + half], src_hi[:, j, c], src_lo[:, j, c],
                                   w_hi[:, c, half * BANK:(half + 1) * BANK],
                                   w_lo[:, c, half * BANK:(half + 1) * BANK], c == 0, c == KD - 1)
                return last

            def rank_within(t):
                pe.wait_ge(chosen_done, nth(t))
                pe.wait_ge(place_done, nth(t - 1))
                nc.tensor.matmul(ps[:, RK, 0:E], k.before[:], both[:], start=True, stop=True)
                nc.tensor.matmul(ps[:, RK, E:2 * E], k.ones_bf[:], both[:], start=True, stop=True)\
                    .then_inc(rank_ps_done, 1)

            pe.wait_ge(src_lo_done, nth(0))
            for a in range(PARTS):
                pe.wait_ge(w_lo_done, nth(a))
                for c in range(KD)[of_part(a)]:
                    for half in range(2):
                        cols = slice(half * BANK, (half + 1) * BANK)
                        last = matmul3(nc, ps[:, half], src_hi[:, 0, c], src_lo[:, 0, c], w_hi[:, c, cols],
                                       w_lo[:, c, cols], c == 0, c == KD - 1)
            last.then_inc(proj_done, 1)
            pe.wait_ge(route_in, nth_dma(1))

            def body(t, j):
                static = isinstance(t, int)
                if not (static and t == NT - 1):
                    project(t + 1, 1 - j, 0)
                pe.wait_ge(norm.h_done, nth(t))
                pe.wait_ge(hT_done, nth(t - 1))
                for c in range(KD):
                    last = nc.tensor.transpose(ps[:, HT_ + c // 4, (c % 4) * P:(c % 4 + 1) * P],
                                               h[:, j, c * P:(c + 1) * P], k.ident[:])
                last.then_inc(hT_ps_done, 1)
                if not (static and t == NT - 1):
                    project(t + 1, 1 - j, 1).then_inc(proj_done, 1)
                pe.wait_ge(hT_done, nth(t))
                pe.wait_ge(chosen_done, nth(t - 1))
                for c in range(KD):
                    last = nc.tensor.matmul(ps[:, LG, 0:W], hT[:, c], w_route[:, c], start=c == 0,
                                            stop=c == KD - 1)
                last.then_inc(logits_done, 1)
                if not (static and t == 0):
                    rank_within(t - 1)

            tiles(pe, body)
            rank_within(NT - 1)
        m.end()


def experts(nc, k, stage, h_rows, ids_dram, w_gate, w_up, w_down, y_rows):
    with ExitStack() as ctx:
        m = Memory(nc, ctx, stage)
        gu_raw = m.sb("gu_raw", [P, 2, KD, 2 * FF])
        wd_raw = m.sb("wd_raw", [P, 2, KF, D])
        gu_hi = m.sb("gu_hi", [P, 2, KD, 2 * FF], F32R)
        gu_lo = m.sb("gu_lo", [P, 2, KD, 2 * FF], F32R)
        wd_hi = m.sb("wd_hi", [P, 2, KF, D], F32R)
        wd_lo = m.sb("wd_lo", [P, 2, KF, D], F32R)
        ids = m.sb("ids", [P, E * SLOTS], I32)
        ids_now = m.sb("ids_now", [P, 1], I32)
        rows = m.sb("rows", [P, D])
        hT_hi = m.sb("hT_hi", [P, KD, P], F32R)
        hT_lo = m.sb("hT_lo", [P, KD, P], F32R)
        silu = m.sb("silu", [P, FF])
        act_ = m.sb("act", [P, FF])
        aT_hi = m.sb("aT_hi", [P, KF, P], F32R)
        aT_lo = m.sb("aT_lo", [P, KF, P], F32R)
        y = m.sb("y", [P, D])

        ps = m.ps("ps", [P, 8, BANK])
        DVE_SHARE = 3
        GU, HT_, AT, Y = 0, 1, 3, 4

        gate_in, up_in, wd_in, ids_in = (m.plain(s) for s in ("gate_in", "up_in", "wd_in", "ids_in"))
        zeroed, table_in = m.plain("zeroed"), m.plain("table_in")
        gu_hi_done, gu_lo_done, gu_lo2_done = (m.sem(s) for s in ("gu_hi_done", "gu_lo_done", "gu_lo2_done"))
        wd_hi_done, wd_lo_done = m.sem("wd_hi_done"), m.sem("wd_lo_done")
        ids_set, rows_in = m.sem("ids_set"), m.plain("rows_in")
        hT_ps_done, hT_hi_done, hT_lo_done = m.sem("hT_ps_done"), m.sem("hT_hi_done"), m.sem("hT_lo_done")
        gu_ps_done, silu_done, act_done = m.sem("gu_ps_done"), m.sem("silu_done"), m.sem("act_done")
        aT_ps_done, aT_hi_done, aT_lo_done = m.sem("aT_ps_done"), m.sem("aT_hi_done"), m.sem("aT_lo_done")
        y_ps_done, y_done, y_stored = m.sem("y_ps_done"), m.sem("y_done"), m.store("y_stored")
        block = m.block()

        def expert_blocks(eng, each, before=None, each_of=None):
            def one(e, at):
                s = eng.value_load(k.block_at[0:1, at], min_val=0, max_val=MAX_BLOCKS - 1)
                n = eng.value_load(k.blocks[0:1, at], min_val=1, max_val=SLOTS)
                with eng.Fori(0, n) as b:
                    (each or each_of(n))(e, b, nc.s_assert_within(s + b, min_val=0, max_val=MAX_BLOCKS - 1))
                return s, n

            with eng.Fori(0, E - 1) as e:
                if before:
                    before(e)
                one(e, bass.ds(e, 1))
            if before:
                before(E - 1)
            s, n = one(E - 1, slice(E - 1, E))
            return nc.s_assert_within(s + n, min_val=1, max_val=MAX_BLOCKS)

        def slot(e):
            return bass.ds(e % 2, 1)

        @block.sync
        def _(sp):
            m.prime(sp)
            sp.dma_start(ids[:], ids_dram.rearrange("(p n) o -> p (n o)", p=P)).then_inc(ids_in, DMA)

            def load(e, landed, into, w):
                if not (isinstance(e, int) and e == 0):
                    sp.wait_ge(landed, nth_dma(e - 1))
                sp.dma_start(into, w[bass.ds(e, 1)].rearrange("e (k p) c -> p e k c", p=P)).then_inc(landed, DMA)

            def load_gu(e):
                load(e, gate_in, gu_raw[:, slot(e), :, 0:FF], w_gate)
                load(e, up_in, gu_raw[:, slot(e), :, FF:], w_up)

            def load_wd(e):
                load(e, wd_in, wd_raw[:, slot(e)], w_down)

            load_gu(0)
            sp.wait_ge(hT_ps_done, nth(0))
            load_wd(0)
            load_gu(1)
            load_wd(1)
            with sp.Fori(0, E - 2) as e:
                sp.wait_ge(gu_lo_done, nth(e))
                sp.wait_ge(gu_lo2_done, nth(e))
                load_gu(e + 2)
                sp.wait_ge(wd_lo_done, nth(e))
                load_wd(e + 2)

        @block.gpsimd
        def _(pool):
            pool.memset(aT_hi[:].bitcast(F32), 0.0)
            pool.memset(aT_lo[:].bitcast(F32), 0.0)
            pool.memset(wd_hi[:, 1].bitcast(F32), 0.0)
            pool.memset(wd_lo[:, 1].bitcast(F32), 0.0).then_inc(zeroed, 1)
            pool.wait_ge(ids_in, nth_dma(0))

            def gather(column, g):
                pool.wait_ge(hT_ps_done, nth(g - 1))
                stand(pool)
                pool.tensor_copy(ids_now[:], ids[:, bass.ds(column, 1)]).then_inc(ids_set, 1)
                pool.wait_ge(ids_set, nth(g))
                stand(pool)
                pool.indirect_dma_start(rows[:], None, h_rows,
                                        bass.IndirectOffsetOnAxis(ids_now[:].bitcast(U32), 0))\
                    .then_inc(rows_in, DMA)

            def split_gu(e):
                pool.wait_ge(gu_hi_done, nth(2 * e))
                stand(pool)
                pool.tensor_tensor(gu_lo[:, slot(e), DVE_SHARE:], gu_raw[:, slot(e), DVE_SHARE:],
                                   gu_hi[:, slot(e), DVE_SHARE:].bitcast(F32), ALU.subtract)\
                    .then_inc(gu_lo2_done, 1)

            def each(n):
                def next_rows(e, b, g):
                    last = 1 - (n - b + (SLOTS - 2)) // SLOTS
                    column = (e * SLOTS + b + 1 + last * (SLOTS - 1 - b)) % (E * SLOTS)
                    gather(nc.s_assert_within(column, min_val=0, max_val=E * SLOTS - 1), g + 1)
                return next_rows

            gather(0, 0)
            blocks = expert_blocks(pool, None, split_gu, each)
            pool.wait_ge(rows_in, nth_dma(blocks))

        @block.scalar
        def _(act):
            def split_gu(e, at):
                act.wait_ge(gate_in, nth_dma(e))
                act.wait_ge(up_in, nth_dma(e))
                stand(act)
                nc.scalar.activation(gu_hi[:, slot(e), at], gu_raw[:, slot(e), at], ACT.Copy)\
                    .then_inc(gu_hi_done, 1)

            def take_rows(g):
                act.wait_ge(hT_ps_done, nth(g))
                for b in range(2):
                    nc.scalar.activation(hT_hi[:, 4 * b:4 * b + 4],
                                         ps[:, HT_ + b].rearrange("p (a c) -> p a c", c=P), ACT.Copy)\
                        .then_inc(hT_hi_done, 1)

            def take_y(g):
                act.wait_ge(y_ps_done, nth(g))
                act.wait_ge(y_stored, nth_store(g - 1))
                nc.scalar.activation(y[:].rearrange("p (b c) -> p b c", b=2), ps[:, Y:Y + 2], ACT.Copy)\
                    .then_inc(y_done, 1)

            def store_y(g):
                act.wait_ge(y_done, nth(g))
                act.dma_start(y_rows[bass.ds(g * P, P), :], y[:]).then_inc(y_stored, DMA)

            act.wait_ge(zeroed, 1)
            nc.scalar.activation(silu[:, 0:1], k.eps[:], ACT.Silu).then_inc(table_in, 1)
            act.wait_ge(table_in, 1)
            split_gu(0, slice(DVE_SHARE, KD))
            split_gu(0, slice(0, DVE_SHARE))
            take_rows(0)

            def before(e):
                if not isinstance(e, int):
                    split_gu(e + 1, slice(DVE_SHARE, KD))
                    split_gu(e + 1, slice(0, DVE_SHARE))

            def each(e, b, g):
                act.wait_ge(gu_ps_done, nth(g))
                act.wait_ge(act_done, nth(g - 1))
                nc.scalar.activation(silu[:], ps[:, GU, 0:FF], ACT.Silu).then_inc(silu_done, 1)
                take_rows(g + 1)
                take_y(g)
                act.wait_ge(aT_ps_done, nth(g))
                nc.scalar.activation(aT_hi[:], ps[:, AT, 0:FF].rearrange("p (a c) -> p a c", c=P), ACT.Copy)\
                    .then_inc(aT_hi_done, 1)
                store_y(g)

            blocks = expert_blocks(act, each, before)
            take_y(blocks)
            store_y(blocks)
            act.wait_ge(y_stored, nth_store(blocks))
            stand(act)

        @block.vector
        def _(dve):
            def split_gu(e):
                dve.wait_ge(gu_hi_done, nth(2 * e + 1))
                nc.vector.tensor_tensor(gu_lo[:, slot(e), 0:DVE_SHARE], gu_raw[:, slot(e), 0:DVE_SHARE],
                                        gu_hi[:, slot(e), 0:DVE_SHARE].bitcast(F32), ALU.subtract)\
                    .then_inc(gu_lo_done, 1)

            def before(e):
                dve.wait_ge(wd_in, nth_dma(e))
                stand(dve)
                nc.vector.tensor_copy(wd_hi[:, slot(e)], wd_raw[:, slot(e)]).then_inc(wd_hi_done, 1)
                dve.wait_ge(wd_hi_done, nth(e))
                nc.vector.tensor_tensor(wd_lo[:, slot(e)], wd_raw[:, slot(e)],
                                        wd_hi[:, slot(e)].bitcast(F32), ALU.subtract).then_inc(wd_lo_done, 1)
                if not isinstance(e, int):
                    split_gu(e + 1)

            def take_rows(g):
                for b in range(2):
                    dve.wait_ge(hT_hi_done, nth(2 * g + b))
                    last = nc.vector.tensor_tensor(
                        hT_lo[:, 4 * b:4 * b + 4], ps[:, HT_ + b].rearrange("p (a c) -> p a c", c=P),
                        hT_hi[:, 4 * b:4 * b + 4].bitcast(F32), ALU.subtract)
                last.then_inc(hT_lo_done, 1)

            dve.wait_ge(zeroed, 1)
            split_gu(0)
            take_rows(0)

            def each(e, b, g):
                dve.wait_ge(silu_done, nth(g))
                nc.vector.tensor_tensor(act_[:], silu[:], ps[:, GU, FF:], ALU.mult).then_inc(act_done, 1)
                take_rows(g + 1)
                dve.wait_ge(aT_hi_done, nth(g))
                nc.vector.tensor_tensor(aT_lo[:], ps[:, AT, 0:FF].rearrange("p (a c) -> p a c", c=P),
                                        aT_hi[:].bitcast(F32), ALU.subtract).then_inc(aT_lo_done, 1)

            expert_blocks(dve, each, before)

        @block.tensor
        def _(pe):
            def transpose_rows(g):
                pe.wait_ge(rows_in, nth_dma(g))
                pe.wait_ge(hT_lo_done, nth(g - 1))
                for c in range(KD):
                    last = nc.tensor.transpose(ps[:, HT_ + c // 4, (c % 4) * P:(c % 4 + 1) * P],
                                               rows[:, c * P:(c + 1) * P], k.ident[:])
                last.then_inc(hT_ps_done, 1)

            def down(g, e):
                pe.wait_ge(aT_lo_done, nth(g - 1))
                pe.wait_ge(wd_lo_done, nth(e))
                pe.wait_ge(y_done, nth(g - 1))
                for half in range(2):
                    cols = slice(half * BANK, (half + 1) * BANK)
                    for c in range(KF):
                        last = matmul3(nc, ps[:, Y + half], aT_hi[:, c], aT_lo[:, c],
                                       wd_hi[:, bass.ds((e + 2) % 2, 1), c, cols],
                                       wd_lo[:, bass.ds((e + 2) % 2, 1), c, cols], c == 0, c == KF - 1)
                last.then_inc(y_ps_done, 1)

            pe.wait_ge(zeroed, 1)
            transpose_rows(0)

            def each(e, b, g):
                pe.wait_ge(gu_lo_done, nth(e))
                pe.wait_ge(gu_lo2_done, nth(e))
                pe.wait_ge(hT_lo_done, nth(g))
                pe.wait_ge(act_done, nth(g - 1))
                for c in range(KD):
                    last = matmul3(nc, ps[:, GU], hT_hi[:, c], hT_lo[:, c], gu_hi[:, slot(e), c],
                                   gu_lo[:, slot(e), c], c == 0, c == KD - 1)
                last.then_inc(gu_ps_done, 1)
                transpose_rows(g + 1)
                down(g, e + ((b + (SLOTS - 1)) // SLOTS) - 1)
                pe.wait_ge(act_done, nth(g))
                pe.wait_ge(aT_lo_done, nth(g - 1))
                for c in range(KF):
                    last = nc.tensor.transpose(ps[:, AT, c * P:(c + 1) * P], act_[:, c * P:(c + 1) * P],
                                               k.ident[:])
                last.then_inc(aT_ps_done, 1)

            blocks = expert_blocks(pe, each)
            down(blocks, E - 1)
        m.end()


class Combine:

    def __init__(self, m, k, x, h, square, y_a, y_b, depth=2):
        self.k, self.y, self.depth = k, (y_a, y_b), depth
        self.norm = Norm(m, k, x, h, square, depth)
        self.row_now = m.sb("row_now", [P, depth, 2], I32)
        self.weight_now = m.sb("weight_now", [P, 2])
        self.row_set = m.sem("row_set")
        self.x_in = [m.plain(f"x_in{j}") for j in range(depth)]
        self.y_in = [m.plain(f"y_in{j}") for j in range(depth)]
        self.x_done = m.sem("x_done")

    def pool(self, nc, pool, y_rows, j, t):
        pool.wait_ge(self.x_done, nth(t - self.depth))
        stand(pool)
        pool.tensor_copy(self.row_now[:, j:j + 1], self.k.row[:, bass.ds(t, 1)]).then_inc(self.row_set, 1)
        pool.wait_ge(self.row_set, nth(t))
        stand(pool)
        for c in range(2):
            pool.indirect_dma_start(self.y[c][:, j], None, y_rows,
                                    bass.IndirectOffsetOnAxis(self.row_now[:, j, c:c + 1].bitcast(U32), 0))\
                .then_inc(self.y_in[j], DMA)

    def scalar(self, nc, act, j, t):
        act.wait_ge(self.x_done, nth(t))
        self.norm.scalar(nc, act, j, t)

    STEPS = 3

    def vector(self, nc, dve, step, j, t, q):
        x = self.norm.x
        stand(dve)
        step(nc.vector.tensor_copy(self.weight_now[:].unsqueeze(1), self.k.weight[:, bass.ds(t, 1)]))
        dve.wait_ge(self.x_in[j], nth_dma(q))
        dve.wait_ge(self.y_in[j], nth_dma(2 * q + 1))
        step(nc.vector.scalar_tensor_tensor(out=x[:, j], in0=self.y[0][:, j], scalar=self.weight_now[:, 0:1],
                                            in1=x[:, j], op0=ALU.mult, op1=ALU.add))
        nc.vector.scalar_tensor_tensor(out=x[:, j], in0=self.y[1][:, j], scalar=self.weight_now[:, 1:2],
                                       in1=x[:, j], op0=ALU.mult, op1=ALU.add).then_inc(self.x_done, 1)


def lru(nc, k, x_dram, y_rows, x_out, norm_w, w_in, conv_w, conv_b, w_r, b_r, w_i, b_i, lam, yT_dram):
    with ExitStack() as ctx:
        m = Memory(nc, ctx, "lru")
        hT_hi = m.sb("hT_hi", [P, KD, TH], F32R)
        hT_lo = m.sb("hT_lo", [P, KD, TH], F32R)
        work = m.sb("work", [P, 4, D])
        shared = m.sb("shared", [P, 4, D])
        square = m.sb("square", [P, D])
        cb = Combine(m, k, work[:, 0:2], work[:, 2:4], square[:], shared[:, 0:2], shared[:, 2:4])
        norm = cb.norm

        def part(at):
            return shared[:, at].rearrange("p (c t) -> p c t", c=LCT)

        r, inp, s_, a = part(0), part(1), part(2), part(3)
        hs = work[:, 3].rearrange("p (c t) -> p c t", c=LCT)
        kinds = []
        for name, shape in (("wx", [P, KD, LBW]), ("wg", [P, KD, LBW]), ("wr", [P, 2, LCT, LBW])):
            kinds.append(dict(raw=m.sb(name + "_raw", shape), hi=m.sb(name + "_hi", shape, F32R),
                              lo=m.sb(name + "_lo", shape, F32R), landed=m.plain(name + "_in"),
                              hi_done=m.sem(name + "_hi_done"), lo_done=m.sem(name + "_lo_done")))
        wx, wg, wr = kinds
        CB, BR, BI, SP, MSP = TAPS, TAPS + 1, TAPS + 2, TAPS + 3, TAPS + 4
        par = m.sb("par", [P, LRU_BLOCKS * LCT, MSP + 1])
        mine = m.sb("mine", [P, LCT, MSP + 1])
        soft = m.sb("soft", [P, LRU_BLOCKS * LCT])
        xb = m.sb("xb", [P, LCT, TAPS - 1 + GROUP])
        xc = m.sb("xc", [P, NG, LCT, GROUP])
        xc_hi = m.sb("xc_hi", [P, NG, LCT, GROUP], F32R)
        xc_lo = m.sb("xc_lo", [P, NG, LCT, GROUP], F32R)
        gate = m.sb("gate", [P, LCT, GROUP])[:], work[:, 2].rearrange("p (c t) -> p c t", c=LCT)
        y = m.sb("y", [P, LCT, GROUP])
        tail = m.sb("tail", [P, LRU_BLOCKS * LCT, TAPS - 1])
        last_h = m.sb("last_h", [P, LRU_BLOCKS * LCT])
        h_start = m.sb("h_start", [P, LCT])

        ps = m.ps("ps", [P, 8, BANK])
        BRANCH, RG, IG = (0, 2), 4, 6

        par_in = m.plain("par_in")
        soft_done = m.plain("soft_done")
        x_stored = [m.store(f"x_stored{j}") for j in range(2)]
        hT_ps_done, hT_hi_done, hT_lo_done = m.sem("hT_ps_done"), m.sem("hT_hi_done"), m.sem("hT_lo_done")
        xb_ps_done, xb_done, conv_done = m.sem("xb_ps_done"), m.sem("xb_done"), m.sem("conv_done")
        xc_hi_done, xc_lo_done = m.sem("xc_hi_done"), m.sem("xc_lo_done")
        gb_ps_done, gate_done = m.sem("gb_ps_done"), m.sem("gate_done")
        rg_ps_done, rg_done, decay_done = m.sem("rg_ps_done"), m.sem("rg_done"), m.sem("decay_done")
        ratio_done, mult_done, y_done = m.sem("ratio_done"), m.sem("mult_done"), m.sem("y_done")
        y_stored = m.store("y_stored")
        order = m.plain("vector_order")
        block = m.block()

        w_rows = w_in.rearrange("(k p) c -> p k c", p=P)
        NBLK = HALVES * LRU_BLOCKS

        @block.sync
        def _(sp):
            m.prime(sp)

            def load(kind, nb):
                if kind is wr:
                    for c, w in enumerate((w_r, w_i)):
                        sp.dma_start(wr["raw"][:, c:c + 1], w[bass.ds(nb, 1)]
                                     .rearrange("n (k p) c -> p n k c", p=P)).then_inc(wr["landed"], DMA)
                else:
                    first = 0 if kind is wx else D
                    sp.dma_start(kind["raw"][:], w_rows[:, :, bass.ds(nb * LBW + first, LBW)])\
                        .then_inc(kind["landed"], DMA)

            for i in range(2):
                sp.dma_start(norm.x[:, i], x_dram[i * P:(i + 1) * P, :]).then_inc(cb.x_in[i], DMA)
            sp.dma_start(norm.norm_w[:], norm_w.partition_broadcast(P)).then_inc(norm.norm_w_in, DMA)
            for half in range(HALVES):
                for i in range(HT):
                    t = half * HT + i
                    sp.wait_ge(cb.x_done, nth(t))
                    sp.dma_start(x_out[bass.ds(t * P, P), :], norm.x[:, i % 2]).then_inc(x_stored[i % 2], DMA)
                    if i < HT - 2:
                        sp.wait_ge(norm.h_done, nth(t))
                        sp.wait_ge(x_stored[i % 2], nth_store(half * (HT // 2) + i // 2))
                        sp.dma_start(norm.x[:, i % 2], x_dram[bass.ds(t * P + 2 * P, P), :])\
                            .then_inc(cb.x_in[i % 2], DMA)
                    if half == 0 and i == 1:
                        load(wx, 0)
                        load(wg, 0)
                    if half == 0 and i == 2:
                        load(wr, 0)
                        with nc.allow_non_contiguous_dma(reason="a few parameters of each channel"):
                            for tap in range(TAPS):
                                sp.dma_start(par[:, :, tap], conv_w[tap].rearrange("(c p) -> p c", p=P)).then_inc(par_in, DMA)
                            for at, v in ((CB, conv_b), (BR, b_r), (BI, b_i), (SP, lam)):
                                sp.dma_start(par[:, :, at], v.rearrange("(c p) -> p c", p=P)).then_inc(par_in, DMA)
                for i in range(2):
                    sp.wait_ge(norm.h_done, nth(half * HT + (HT - 2 + i)))
                    sp.wait_ge(x_stored[i], nth_store(half * (HT // 2) + (HT // 2 - 1)))
                    sp.dma_start(norm.x[:, i], x_dram[bass.ds(((half + 1) % HALVES) * TH + i * P, P), :])\
                        .then_inc(cb.x_in[i], DMA)
                with sp.Fori(0, LRU_BLOCKS) as b:
                    n = half * LRU_BLOCKS + b
                    for kind in kinds:
                        sp.wait_ge(kind["lo_done"], nth(n))
                        load(kind, (b + 1) % LRU_BLOCKS)
                    for g in range(NG):
                        sp.wait_ge(y_done, nth(n * NG + g))
                        sp.dma_start(yT_dram[bass.ds(b * LBW, LBW), bass.ds(half * TH + g * GROUP, GROUP)]
                                     .rearrange("(c p) t -> p c t", p=P), y[:]).then_inc(y_stored, DMA)
            sp.wait_ge(y_stored, nth_store(NBLK * NG - 1))
            sp.wait_ge(wx["landed"], nth_dma(NBLK))
            sp.wait_ge(wg["landed"], nth_dma(NBLK))
            sp.wait_ge(wr["landed"], nth_dma(2 * NBLK + 1))
            for i in range(2):
                sp.wait_ge(cb.x_in[i], nth_dma(NT // 2))

        @block.gpsimd
        def _(pool):
            with pool.Fori(0, HALVES) as half:
                pool.wait_ge(y_done, nth(half * (LRU_BLOCKS * NG) - 1))
                stand(pool)
                for i in range(HT):
                    cb.pool(nc, pool, y_rows, i % 2, half * HT + i)

        @block.scalar
        def _(act):
            def split(kind, n):
                act.wait_ge(kind["landed"], nth_dma(2 * n + 1 if kind is wr else n))
                nc.scalar.activation(kind["hi"][:], kind["raw"][:], ACT.Copy).then_inc(kind["hi_done"], 1)

            for half in range(HALVES):
                cb.scalar(nc, act, 0, half * HT)
                for i in range(HT):
                    t = half * HT + i
                    act.wait_ge(hT_ps_done, nth(t))
                    for b in range(2):
                        nc.scalar.activation(hT_hi[:, 4 * b:4 * b + 4, i * P:(i + 1) * P],
                                             ps[:, 2 * (i % 2) + b].rearrange("p (a c) -> p a c", c=P),
                                             ACT.Copy).then_inc(hT_hi_done, 1)
                    if i + 1 < HT:
                        cb.scalar(nc, act, (i + 1) % 2, t + 1)
                    if half == 0 and i >= HT - len(kinds):
                        split(kinds[i - HT], 0)
                    if half == 0 and i == HT - 1:
                        act.wait_ge(par_in, nth_dma(TAPS + 3))
                        nc.scalar.activation(soft[:], par[:, :, SP], ACT.Abs).then_inc(soft_done, 1)
                        act.wait_ge(soft_done, 1)
                        nc.scalar.activation(soft[:], soft[:], ACT.Exp, scale=-1.0).then_inc(soft_done, 1)
                        act.wait_ge(soft_done, 2)
                        nc.scalar.activation(soft[:], soft[:], ACT.Ln, bias=1.0).then_inc(soft_done, 1)
                with act.Fori(0, LRU_BLOCKS) as b:
                    n = half * LRU_BLOCKS + b
                    q0 = n * NG

                    def take_xb(g):
                        act.wait_ge(xb_ps_done, nth(q0 + g))
                        act.wait_ge(conv_done, nth(q0 + g - 1))
                        nc.scalar.activation(xb[:, :, TAPS - 1:], ps[:, BRANCH[g]:BRANCH[g] + 2], ACT.Copy)\
                            .then_inc(xb_done, 1)

                    def take_xc(g):
                        act.wait_ge(conv_done, nth(q0 + g))
                        act.wait_ge(rg_ps_done, nth(q0 + g - NG))
                        nc.scalar.activation(xc_hi[:, g], xc[:, g], ACT.Copy).then_inc(xc_hi_done, 1)

                    def take_gate(g):
                        act.wait_ge(gb_ps_done, nth(q0 + g))
                        act.wait_ge(y_done, nth(q0 + g - NG))
                        nc.scalar.activation(gate[g], ps[:, BRANCH[g]:BRANCH[g] + 2], ACT.Gelu_apprx_tanh)\
                            .then_inc(gate_done, 1)

                    def decays(g):
                        q = q0 + g
                        act.wait_ge(rg_ps_done, nth(q))
                        act.wait_ge(decay_done, nth(q - 1))
                        act.wait_ge(y_done, nth(q - 1))
                        for c in range(LCT):
                            nc.scalar.activation(r[:, c], ps[:, RG + c], ACT.Sigmoid, bias=mine[:, c, BR:BR + 1])
                            last = nc.scalar.activation(inp[:, c], ps[:, IG + c], ACT.Sigmoid,
                                                        bias=mine[:, c, BI:BI + 1])
                        last.then_inc(rg_done, 1)
                        act.wait_ge(rg_done, nth(q))
                        for c in range(LCT):
                            nc.scalar.activation(s_[:, c], r[:, c], ACT.Tanh, scale=mine[:, c, SP:SP + 1])
                        for c in range(LCT):
                            last = nc.scalar.activation(a[:, c], r[:, c], ACT.Exp, scale=mine[:, c, MSP:MSP + 1])
                        last.then_inc(decay_done, 1)

                    def root(g):
                        act.wait_ge(ratio_done, nth(q0 + g))
                        nc.scalar.activation(s_, s_, ACT.Sqrt).then_inc(mult_done, 1)

                    take_xb(0)
                    take_xc(0)
                    take_xb(1)
                    split(wx, n + 1)
                    take_gate(0)
                    take_xc(1)
                    decays(0)
                    take_gate(1)
                    split(wg, n + 1)
                    root(0)
                    decays(1)
                    split(wr, n + 1)
                    root(1)

        @block.vector
        def _(dve):
            step = Steps(dve, order)
            step.add(nc.vector.memset(tail[:], 0.0))
            step.add(nc.vector.memset(last_h[:], 0.0))
            step.wait()
            dve.wait_ge(norm.norm_w_in, nth_dma(0))

            def split(kind, n):
                dve.wait_ge(kind["hi_done"], nth(n))
                nc.vector.tensor_tensor(kind["lo"][:], kind["raw"][:], kind["hi"][:].bitcast(F32), ALU.subtract)\
                    .then_inc(kind["lo_done"], 1)

            IN_BLOCK = LRU_STEPS
            for half in range(HALVES):

                def combine(i):
                    cb.vector(nc, dve, step, i % 2, half * HT + i, half * (HT // 2) + i // 2)

                def normalise(i):
                    dve.wait_ge(hT_ps_done, nth(half * HT + i - 2))
                    norm.vector(nc, dve, step, i % 2, half * HT + i)

                combine(0)
                normalise(0)
                for i in range(HT):
                    t = half * HT + i
                    if i + 1 < HT:
                        combine(i + 1)
                    for b in range(2):
                        dve.wait_ge(hT_hi_done, nth(2 * t + b))
                        at = (slice(None), slice(4 * b, 4 * b + 4), slice(i * P, (i + 1) * P))
                        last = nc.vector.tensor_tensor(
                            hT_lo[at], ps[:, 2 * (i % 2) + b].rearrange("p (a c) -> p a c", c=P),
                            hT_hi[at].bitcast(F32), ALU.subtract)
                    last.then_inc(hT_lo_done, 1)
                    if i + 1 < HT:
                        normalise(i + 1)
                    if half == 0 and i >= HT - len(kinds):
                        split(kinds[i - HT], 0)
                    if half == 0 and i == HT - 1:
                        dve.wait_ge(par_in, nth_dma(TAPS + 3))
                        dve.wait_ge(soft_done, 3)
                        step(nc.vector.tensor_scalar(par[:, :, SP], par[:, :, SP], -1.0, 0.0, ALU.mult, ALU.max))
                        step(nc.vector.tensor_tensor(par[:, :, SP], par[:, :, SP], soft[:], ALU.add))
                        step(nc.vector.tensor_scalar(par[:, :, MSP], par[:, :, SP], -LRU_C, None, ALU.mult))
                        step(nc.vector.tensor_scalar(par[:, :, SP], par[:, :, SP], LRU_C, None, ALU.mult))
                before = step.base + step.n
                with dve.Fori(0, LRU_BLOCKS) as b:
                    n = half * LRU_BLOCKS + b
                    step.loop(b * IN_BLOCK + before)
                    channels = bass.ds(b * LCT, LCT)
                    stand(dve)
                    step(nc.vector.tensor_copy(mine[:], par[:, channels]))

                    def convolve(g):
                        q = n * NG + g
                        stand(dve)
                        step.add(nc.vector.tensor_copy(xb[:, :, 0:TAPS - 1], tail[:, channels]))
                        dve.wait_ge(xb_done, nth(q))
                        step.wait()
                        for c in range(LCT):
                            step.add(nc.vector.tensor_scalar(
                                xc[:, g, c], xb[:, c, 0:GROUP], mine[:, c, 0:1], mine[:, c, CB:CB + 1],
                                ALU.mult, ALU.add))
                        step.add(nc.vector.tensor_copy(tail[:, channels], xb[:, :, GROUP:]))
                        step.wait()
                        for tap in range(1, TAPS):
                            for c in range(LCT):
                                last = nc.vector.scalar_tensor_tensor(
                                    out=xc[:, g, c], in0=xb[:, c, tap:tap + GROUP],
                                    scalar=mine[:, c, tap:tap + 1], in1=xc[:, g, c], op0=ALU.mult, op1=ALU.add)
                                if tap < TAPS - 1:
                                    step.add(last)
                            if tap < TAPS - 1:
                                step.wait()
                        last.then_inc(conv_done, 1)

                    def take_xc(g):
                        dve.wait_ge(xc_hi_done, nth(n * NG + g))
                        nc.vector.tensor_tensor(xc_lo[:, g], xc[:, g], xc_hi[:, g].bitcast(F32), ALU.subtract)\
                            .then_inc(xc_lo_done, 1)

                    def recur(g, between):
                        q = n * NG + g
                        stand(dve)
                        step.add(nc.vector.tensor_copy(h_start[:].unsqueeze(2), last_h[:, channels].unsqueeze(2)))
                        dve.wait_ge(rg_done, nth(q))
                        step.add(nc.vector.tensor_tensor(inp, inp, xc[:, g], ALU.mult))
                        dve.wait_ge(decay_done, nth(q))
                        dve.wait_ge(y_stored, nth_store(q - 1))
                        step(nc.vector.tensor_tensor(y[:], a, a, ALU.mult))
                        step(nc.vector.tensor_scalar(y[:], y[:], 1.0, None, ALU.add))
                        nc.vector.scalar_tensor_tensor(out=s_, in0=s_, scalar=2.0 ** -116, in1=y[:],
                                                       op0=ALU.max, op1=ALU.mult).then_inc(ratio_done, 1)
                        between()
                        dve.wait_ge(mult_done, nth(q))
                        step(nc.vector.tensor_tensor(inp, inp, s_, ALU.mult))
                        for c in range(LCT):
                            step.add(nc.vector.tensor_tensor_scan(hs[:, c], a[:, c], inp[:, c],
                                                                  h_start[:, c:c + 1], ALU.mult, ALU.add))
                        dve.wait_ge(gate_done, nth(q))
                        step.wait()
                        nc.vector.tensor_tensor(y[:], hs, gate[g], ALU.mult).then_inc(y_done, 1)
                        step.add(nc.vector.tensor_copy(last_h[:, channels].unsqueeze(2), hs[:, :, GROUP - 1:]))
                        step.wait()
                        dve.wait_ge(y_done, nth(q))

                    convolve(0)
                    take_xc(0)
                    dve.wait_ge(conv_done, nth(n * NG))
                    convolve(1)
                    split(wx, n + 1)
                    take_xc(1)
                    recur(0, lambda: None)
                    split(wg, n + 1)
                    recur(1, lambda: split(wr, n + 1))
                    assert step.n == IN_BLOCK, step.n
                step.after(before + LRU_BLOCKS * IN_BLOCK)

        @block.tensor
        def _(pe):
            with pe.Fori(0, HALVES) as half:
                for i in range(HT):
                    t = half * HT + i
                    if i == 0:
                        pe.wait_ge(gate_done, nth(half * (LRU_BLOCKS * NG) - 1))
                    pe.wait_ge(hT_lo_done, nth(t - 2))
                    pe.wait_ge(norm.h_done, nth(t))
                    for c in range(KD):
                        last = nc.tensor.transpose(ps[:, 2 * (i % 2) + c // 4, (c % 4) * P:(c % 4 + 1) * P],
                                                   norm.h[:, i % 2, c * P:(c + 1) * P], k.ident[:])
                    last.then_inc(hT_ps_done, 1)
                pe.wait_ge(hT_lo_done, nth(half * HT + (HT - 1)))
                stand(pe)
                with pe.Fori(0, LRU_BLOCKS) as b:
                    n = half * LRU_BLOCKS + b

                    def branch(kind, g, done):
                        cols = slice(g * GROUP, (g + 1) * GROUP)
                        for o in range(LCT):
                            at = slice(o * P, (o + 1) * P)
                            for c in range(KD):
                                last = matmul3(nc, ps[:, BRANCH[g] + o], kind["hi"][:, c, at],
                                               kind["lo"][:, c, at], hT_hi[:, c, cols],
                                               hT_lo[:, c, cols], c == 0, c == KD - 1)
                        last.then_inc(done, 1)

                    def gates(g):
                        q = n * NG + g
                        pe.wait_ge(xc_lo_done, nth(q))
                        pe.wait_ge(rg_done, nth(q - 1))
                        for which, bank in ((0, RG), (1, IG)):
                            for o in range(LCT):
                                at = slice(o * P, (o + 1) * P)
                                for c in range(LCT):
                                    last = matmul3(nc, ps[:, bank + o], wr["hi"][:, which, c, at],
                                                   wr["lo"][:, which, c, at], xc_hi[:, g, c], xc_lo[:, g, c],
                                                   c == 0, c == LCT - 1)
                        last.then_inc(rg_ps_done, 1)

                    pe.wait_ge(wx["lo_done"], nth(n))
                    for g in range(NG):
                        pe.wait_ge(gate_done, nth((n - 1) * NG + g))
                        branch(wx, g, xb_ps_done)
                    pe.wait_ge(wg["lo_done"], nth(n))
                    pe.wait_ge(wr["lo_done"], nth(n))
                    for g in range(NG):
                        pe.wait_ge(xb_done, nth(n * NG + g))
                        branch(wg, g, gb_ps_done)
                        gates(g)
        m.end()


def finish(nc, k, x_dram, y_rows, norm_w, out):
    DEPTH = 4
    with ExitStack() as ctx:
        m = Memory(nc, ctx, "finish")
        x = m.sb("x", [P, DEPTH, D])
        h = m.sb("h", [P, DEPTH, D])
        square = m.sb("square", [P, D])
        y_a, y_b = m.sb("y_a", [P, DEPTH, D]), m.sb("y_b", [P, DEPTH, D])
        cb = Combine(m, k, x, h, square[:], y_a, y_b, DEPTH)
        stored = [m.store(f"stored{j}") for j in range(DEPTH)]
        order = m.plain("vector_order")
        block = m.block()

        def tiles(eng, body):
            with eng.Fori(0, NT // DEPTH) as q:
                for j in range(DEPTH):
                    body(j, q * DEPTH + j, q)

        @block.sync
        def _(sp):
            m.prime(sp)

            def load(j, t, q):
                sp.wait_ge(cb.norm.h_done, nth(t - DEPTH))
                sp.dma_start(x[:, j], x_dram[bass.ds(t * P, P), :]).then_inc(cb.x_in[j], DMA)

            sp.dma_start(cb.norm.norm_w[:], norm_w.partition_broadcast(P)).then_inc(cb.norm.norm_w_in, DMA)
            tiles(sp, load)

        @block.gpsimd
        def _(pool):
            tiles(pool, lambda j, t, q: cb.pool(nc, pool, y_rows, j, t))

        @block.scalar
        def _(act):
            def body(j, t, q):
                cb.scalar(nc, act, j, t)
                act.wait_ge(cb.norm.h_done, nth(t))
                act.dma_start(out[bass.ds(t * P, P), :], h[:, j]).then_inc(stored[j], DMA)

            tiles(act, body)
            for j in range(DEPTH):
                act.wait_ge(stored[j], nth_store(NT // DEPTH - 1))

        @block.vector
        def _(dve):
            step = Steps(dve, order)
            dve.wait_ge(cb.norm.norm_w_in, nth_dma(0))

            def body(j, t, q):
                if j == 0:
                    step.loop(q * (DEPTH * Combine.STEPS))
                cb.vector(nc, dve, step, j, t, q)
                dve.wait_ge(stored[j], nth_store(q - 1))
                cb.norm.vector(nc, dve, step, j, t)

            tiles(dve, body)
        m.end()


def build(nc, x, gla_norm, gla_w_in, gla_w_alpha, gla_b_alpha, gla_head_norm, gla_w_out,
          lru_norm, lru_w_in, lru_conv_w, lru_conv_b, lru_w_rgate, lru_b_rgate, lru_w_igate,
          lru_b_igate, lru_lambda, lru_w_out, moe_norm, moe_w_group, moe_w_expert, moe_w_gate,
          moe_w_up, moe_w_down, final_norm, out):
    def scratch(name, shape, dt=F32):
        return nc.dram_tensor(name, shape, dt, kind="Internal").ap()

    oT = scratch("oT_rows", [D, T])
    x1, x2, x3 = (scratch(f"x{n}_rows", [T, D]) for n in (1, 2, 3))
    h_rows = scratch("h_rows", [T, D])
    y_rows = scratch("y_rows", [(MAX_BLOCKS + 1) * P, D])
    ids = scratch("gather_lists", [P * E * SLOTS, 1], I32)
    with ExitStack() as ctx:
        k = Consts(nc, ctx)
        constants(nc, k)
        gla(nc, k, x[0], gla_norm[0], gla_w_in[0], gla_w_alpha[0], gla_b_alpha[0], gla_head_norm[0], oT,
            y_rows[(MIN_BLOCKS + 1) * P:, :])
        project_and_route(nc, k, "route0", oT, gla_w_out[0], x[0], x1, h_rows, moe_norm[0],
                          moe_w_group[0], moe_w_expert[0], ids)
        experts(nc, k, "experts0", h_rows, ids, moe_w_gate[0], moe_w_up[0], moe_w_down[0], y_rows)
        lru(nc, k, x1, y_rows, x2, lru_norm[0], lru_w_in[0], lru_conv_w[0], lru_conv_b[0],
            lru_w_rgate[0], lru_b_rgate[0], lru_w_igate[0], lru_b_igate[0], lru_lambda[0], oT)
        project_and_route(nc, k, "route1", oT, lru_w_out[0], x2, x3, h_rows, moe_norm[1],
                          moe_w_group[1], moe_w_expert[1], ids)
        experts(nc, k, "experts1", h_rows, ids, moe_w_gate[1], moe_w_up[1], moe_w_down[1], y_rows)
        finish(nc, k, x3, y_rows, final_norm, out[0])


INPUTS = ["x", "gla_norm", "gla_w_in", "gla_w_alpha", "gla_b_alpha", "gla_head_norm", "gla_w_out",
          "lru_norm", "lru_w_in", "lru_conv_w", "lru_conv_b", "lru_w_rgate", "lru_b_rgate",
          "lru_w_igate", "lru_b_igate", "lru_lambda", "lru_w_out", "moe_norm", "moe_w_group",
          "moe_w_expert", "moe_w_gate", "moe_w_up", "moe_w_down", "final_norm"]


def kernel(**inputs):
    import numpy as np
    import concourse.bacc as bacc
    from concourse.bass_utils import run_bass_kernel_spmd

    nc = bacc.Bacc("TRN2", target_bir_lowering=False, num_devices=1)
    arrays, args = {}, []
    for name in INPUTS:
        a = np.ascontiguousarray(inputs[name])
        arrays[f"in_{name}"] = a
        args.append(nc.dram_tensor(f"in_{name}", a.shape, mybir.dt.from_np(a.dtype), kind="ExternalInput").ap())
    out = nc.dram_tensor("out", (1, T, D), F32, kind="ExternalOutput").ap()
    build(nc, *args, out)
    r = run_bass_kernel_spmd(nc, [arrays], core_ids=[0])
    return r.results[0]["out"]
```
